# Optimizing a Trainium2 kernel written in Bass

```python
import math
import jax
import jax.numpy as jnp
from jax import lax
import numpy as np

D_MODEL = 1024
BATCH = 1
SEQ = 256
DEPTH = 2

N_DIFF_HEADS = 8
DIFF_HEAD_DIM = D_MODEL // N_DIFF_HEADS // 2
ROPE_THETA = 10000.0
Q_BLOCK = 128
D_RNN = D_MODEL
N_LRU_BLOCKS = 8
LRU_BLOCK = D_RNN // N_LRU_BLOCKS
CONV_WIDTH = 4
LRU_C = 8.0
D_FF = 2816
N_EXPERTS = 8
TOP_K = 2
D_FF_EXPERT = 3584
EXPERT_BLOCK = 256
D_PLE = 256
NORM_EPS = 1e-6
SUBLN_EPS = 1e-5

kernel_name = 'hybrid_diffattn_rglru_moe'

def rmsnorm(x, g, eps=NORM_EPS):
    xf = x.astype(jnp.float32)
    y = xf * lax.rsqrt(jnp.mean(xf * xf, axis=-1, keepdims=True) + eps)
    return (y * g.astype(jnp.float32)).astype(x.dtype)

def rope_tables(seq, dim):
    inv = 1.0 / (ROPE_THETA ** (jnp.arange(0, dim, 2, dtype=jnp.float32) / dim))
    ang = jnp.arange(seq, dtype=jnp.float32)[:, None] * inv[None, :]
    return jnp.cos(ang), jnp.sin(ang)

def apply_rope(x, cos, sin):
    x1, x2 = jnp.split(x.astype(jnp.float32), 2, axis=-1)
    c = cos[None, :, None, :]
    s = sin[None, :, None, :]
    return jnp.concatenate([x1 * c - x2 * s, x2 * c + x1 * s], axis=-1).astype(x.dtype)

def diff_attention(xn, wq, wk, wv, wo, lq1, lk1, lq2, lk2, subln_g, lambda_init):
    B, S, _ = xn.shape
    H, d = N_DIFF_HEADS, DIFF_HEAD_DIM
    q = (xn @ wq).reshape(B, S, 2 * H, d)
    k = (xn @ wk).reshape(B, S, 2 * H, d)
    v = (xn @ wv).reshape(B, S, H, 2 * d)
    cos, sin = rope_tables(S, d)
    q = apply_rope(q, cos, sin) * (d ** -0.5)
    k = apply_rope(k, cos, sin)
    lam = (jnp.exp(jnp.sum(lq1.astype(jnp.float32) * lk1.astype(jnp.float32)))
           - jnp.exp(jnp.sum(lq2.astype(jnp.float32) * lk2.astype(jnp.float32)))
           + lambda_init)
    outs = []
    for start in range(0, S, Q_BLOCK):
        end = start + Q_BLOCK
        qb = q[:, start:end]
        kb = k[:, :end]
        vb = v[:, :end]
        s = jnp.einsum('bqmd,bkmd->bmqk', qb, kb, preferred_element_type=jnp.float32)
        qpos = jnp.arange(start, end)[:, None]
        kpos = jnp.arange(end)[None, :]
        s = jnp.where(kpos <= qpos, s, -jnp.inf)
        w = jax.nn.softmax(s, axis=-1).reshape(B, H, 2, Q_BLOCK, end)
        wdiff = w[:, :, 0] - lam * w[:, :, 1]
        outs.append(jnp.einsum('bhqk,bkhe->bqhe', wdiff.astype(vb.dtype), vb))
    o = jnp.concatenate(outs, axis=1)
    o = rmsnorm(o, subln_g, SUBLN_EPS) * (1.0 - lambda_init)
    return o.reshape(B, S, H * 2 * d) @ wo

def block_diag_linear(x, w, b):
    B, S, C = x.shape
    xb = x.reshape(B, S, N_LRU_BLOCKS, LRU_BLOCK)
    return jnp.einsum('bsnc,ncd->bsnd', xb, w).reshape(B, S, C) + b

def causal_depthwise_conv(x, w, b):
    C = x.shape[-1]
    y = lax.conv_general_dilated(
        x, w[:, None, :], window_strides=(1,), padding=[(CONV_WIDTH - 1, 0)],
        dimension_numbers=('NWC', 'WIO', 'NWC'), feature_group_count=C)
    return y + b

def rg_lru(x, wa, ba, wx, bx, lam):
    r = jax.nn.sigmoid(block_diag_linear(x, wa, ba)).astype(jnp.float32)
    i = jax.nn.sigmoid(block_diag_linear(x, wx, bx)).astype(jnp.float32)
    log_a = -LRU_C * r * jax.nn.softplus(-lam.astype(jnp.float32))
    a = jnp.exp(log_a)
    mult = jnp.sqrt(-jnp.expm1(2.0 * log_a))
    bt = mult * i * x.astype(jnp.float32)

    def combine(left, right):
        a1, b1 = left
        a2, b2 = right
        return a1 * a2, a2 * b1 + b2

    _, h = lax.associative_scan(combine, (a, bt), axis=1)
    return h.astype(x.dtype)

def recurrent_block(xn, w_in_x, w_in_y, conv_w, conv_b, wa, ba, wx, bx, lam, w_out):
    y = jax.nn.gelu(xn @ w_in_y, approximate=True)
    u = causal_depthwise_conv(xn @ w_in_x, conv_w, conv_b)
    h = rg_lru(u, wa, ba, wx, bx, lam)
    return (h * y) @ w_out

def swiglu(xn, wg, wu, wd):
    return (jax.nn.silu(xn @ wg) * (xn @ wu)) @ wd

def moe_swiglu(xn, w_router, w_gate, w_up, w_down):
    B, S, D = xn.shape
    N = B * S
    xt = xn.reshape(N, D)
    logits = jnp.einsum('nd,de->ne', xt, w_router, preferred_element_type=jnp.float32)
    top_vals, top_idx = lax.top_k(logits, TOP_K)
    gates = jax.nn.softmax(top_vals, axis=-1)
    flat_e = top_idx.reshape(-1).astype(jnp.int32)
    flat_tok = jnp.repeat(jnp.arange(N, dtype=jnp.int32), TOP_K)
    flat_g = gates.reshape(-1)
    order = jnp.argsort(flat_e, stable=True)
    sorted_e = flat_e[order]
    counts = jnp.bincount(flat_e, length=N_EXPERTS).astype(jnp.int32)
    padded = (counts + EXPERT_BLOCK - 1) // EXPERT_BLOCK * EXPERT_BLOCK
    start = jnp.cumsum(counts) - counts
    pstart = jnp.cumsum(padded) - padded
    rank = jnp.arange(N * TOP_K, dtype=jnp.int32) - start[sorted_e]
    dest = pstart[sorted_e] + rank
    n_blocks = -(-(N * TOP_K) // EXPERT_BLOCK) + N_EXPERTS
    P = n_blocks * EXPERT_BLOCK
    slot_tok = jnp.zeros((P,), jnp.int32).at[dest].set(flat_tok[order])
    slot_gate = jnp.zeros((P,), jnp.float32).at[dest].set(flat_g[order])
    block_start = jnp.arange(n_blocks, dtype=jnp.int32) * EXPERT_BLOCK
    block_expert = jnp.minimum(
        jnp.searchsorted(jnp.cumsum(padded), block_start, side='right'), N_EXPERTS - 1)
    xs = xt[slot_tok].reshape(n_blocks, EXPERT_BLOCK, D)

    def expert_block(args):
        xb, e = args
        hb = jax.nn.silu(xb @ w_gate[e]) * (xb @ w_up[e])
        return hb @ w_down[e]

    ys = lax.map(expert_block, (xs, block_expert)).reshape(P, D)
    out = jnp.zeros((N, D), jnp.float32).at[slot_tok].add(
        ys.astype(jnp.float32) * slot_gate[:, None])
    return out.astype(xn.dtype).reshape(B, S, D)

def per_layer_embedding(h, p_i, ln_g, w_proj, w_gate):
    g = jax.nn.sigmoid(rmsnorm(h, ln_g) @ w_gate)
    return g * (p_i @ w_proj)

def setup_inputs(seed: int = 0) -> dict:
    key = jax.random.key(seed)
    ks = jax.random.split(key, 40)
    n_even = (DEPTH + 1) // 2
    n_odd = DEPTH // 2
    D = D_MODEL
    d = DIFF_HEAD_DIM
    f32 = jnp.float32

    def nrm(k, shape, fan_in):
        return jax.random.normal(k, shape, f32) * (fan_in ** -0.5)

    def gain(k, shape):
        return 1.0 + 0.02 * jax.random.normal(k, shape, f32)

    def bias(k, shape):
        return 0.01 * jax.random.normal(k, shape, f32)

    a0 = jax.random.uniform(ks[27], (n_odd, D_RNN), f32, 0.9, 0.999)
    s0 = a0 ** (1.0 / LRU_C)
    lru_lambda = jnp.log(s0) - jnp.log1p(-s0)

    return {
        'x': jax.random.normal(ks[0], (BATCH, SEQ, D), f32),
        'p': jax.random.normal(ks[1], (DEPTH, BATCH, SEQ, D_PLE), f32),
        'ln_mix': gain(ks[2], (DEPTH, D)),
        'ln_ffn': gain(ks[3], (DEPTH, D)),
        'ln_ple': gain(ks[4], (DEPTH, D)),
        'ln_final': gain(ks[5], (D,)),
        'ple_w_proj': nrm(ks[6], (DEPTH, D_PLE, D), D_PLE),
        'ple_w_gate': nrm(ks[7], (DEPTH, D, D), D),
        'attn_wq': nrm(ks[8], (n_even, D, 2 * N_DIFF_HEADS * d), D),
        'attn_wk': nrm(ks[9], (n_even, D, 2 * N_DIFF_HEADS * d), D),
        'attn_wv': nrm(ks[10], (n_even, D, 2 * N_DIFF_HEADS * d), D),
        'attn_wo': nrm(ks[11], (n_even, 2 * N_DIFF_HEADS * d, D), 2 * N_DIFF_HEADS * d),
        'attn_lambda_q1': 0.1 * jax.random.normal(ks[12], (n_even, d), f32),
        'attn_lambda_k1': 0.1 * jax.random.normal(ks[13], (n_even, d), f32),
        'attn_lambda_q2': 0.1 * jax.random.normal(ks[14], (n_even, d), f32),
        'attn_lambda_k2': 0.1 * jax.random.normal(ks[15], (n_even, d), f32),
        'attn_subln': gain(ks[16], (n_even, 2 * d)),
        'ffn_w_gate': nrm(ks[17], (n_even, D, D_FF), D),
        'ffn_w_up': nrm(ks[18], (n_even, D, D_FF), D),
        'ffn_w_down': nrm(ks[19], (n_even, D_FF, D), D_FF),
        'lru_w_in_x': nrm(ks[20], (n_odd, D, D_RNN), D),
        'lru_w_in_y': nrm(ks[21], (n_odd, D, D_RNN), D),
        'lru_conv_w': nrm(ks[22], (n_odd, CONV_WIDTH, D_RNN), CONV_WIDTH),
        'lru_conv_b': bias(ks[23], (n_odd, D_RNN)),
        'lru_gate_a_w': nrm(ks[24], (n_odd, N_LRU_BLOCKS, LRU_BLOCK, LRU_BLOCK), LRU_BLOCK),
        'lru_gate_a_b': bias(ks[25], (n_odd, D_RNN)),
        'lru_gate_x_w': nrm(ks[26], (n_odd, N_LRU_BLOCKS, LRU_BLOCK, LRU_BLOCK), LRU_BLOCK),
        'lru_gate_x_b': bias(ks[28], (n_odd, D_RNN)),
        'lru_lambda': lru_lambda,
        'lru_w_out': nrm(ks[29], (n_odd, D_RNN, D), D_RNN),
        'moe_w_router': nrm(ks[30], (n_odd, D, N_EXPERTS), D),
        'moe_w_gate': nrm(ks[31], (n_odd, N_EXPERTS, D, D_FF_EXPERT), D),
        'moe_w_up': nrm(ks[32], (n_odd, N_EXPERTS, D, D_FF_EXPERT), D),
        'moe_w_down': nrm(ks[33], (n_odd, N_EXPERTS, D_FF_EXPERT, D), D_FF_EXPERT),
    }

def reference(x, p, ln_mix, ln_ffn, ln_ple, ln_final, ple_w_proj, ple_w_gate,
              attn_wq, attn_wk, attn_wv, attn_wo, attn_lambda_q1, attn_lambda_k1,
              attn_lambda_q2, attn_lambda_k2, attn_subln,
              ffn_w_gate, ffn_w_up, ffn_w_down,
              lru_w_in_x, lru_w_in_y, lru_conv_w, lru_conv_b, lru_gate_a_w, lru_gate_a_b,
              lru_gate_x_w, lru_gate_x_b, lru_lambda, lru_w_out,
              moe_w_router, moe_w_gate, moe_w_up, moe_w_down):
    h = x
    for i in range(DEPTH):
        j = i // 2
        hn = rmsnorm(h, ln_mix[i])
        if i % 2 == 0:
            lambda_init = 0.8 - 0.6 * math.exp(-0.3 * i)
            h = h + diff_attention(hn, attn_wq[j], attn_wk[j], attn_wv[j], attn_wo[j],
                                   attn_lambda_q1[j], attn_lambda_k1[j],
                                   attn_lambda_q2[j], attn_lambda_k2[j],
                                   attn_subln[j], lambda_init)
            h = h + swiglu(rmsnorm(h, ln_ffn[i]), ffn_w_gate[j], ffn_w_up[j], ffn_w_down[j])
        else:
            h = h + recurrent_block(hn, lru_w_in_x[j], lru_w_in_y[j], lru_conv_w[j], lru_conv_b[j],
                                    lru_gate_a_w[j], lru_gate_a_b[j], lru_gate_x_w[j],
                                    lru_gate_x_b[j], lru_lambda[j], lru_w_out[j])
            h = h + moe_swiglu(rmsnorm(h, ln_ffn[i]), moe_w_router[j], moe_w_gate[j],
                               moe_w_up[j], moe_w_down[j])
        h = h + per_layer_embedding(h, p[i], ln_ple[i], ple_w_proj[i], ple_w_gate[i])
    return rmsnorm(h, ln_final)


_drawn_inputs = setup_inputs


def setup_inputs(seed=0):
    import zlib

    import numpy as np

    out = dict(_drawn_inputs(seed))
    spreads = {}
    factors = {'ln_ple': 20.081,
     'ln_final': 7.299,
     'attn_lambda_q2': 3.35,
     'lru_conv_b': 2.765,
     'lru_gate_a_b': 43.384,
     'lru_gate_x_b': 25.145}
    for name, (base, spread) in spreads.items():
        noise = np.random.default_rng([zlib.crc32(name.encode()), seed]).standard_normal(out[name].shape)
        drawn = base * np.exp(spread * noise) if base else spread * noise
        out[name] = jnp.asarray(drawn.astype(out[name].dtype))
    for name, factor in factors.items():
        out[name] = (out[name] * factor).astype(out[name].dtype)
    return out
```

```python
import math
from contextlib import ExitStack

import numpy as np
import concourse.bass as bass
from concourse import mybir

F32 = mybir.dt.float32
F32R = mybir.dt.float32r
I32 = mybir.dt.int32
ALU = mybir.AluOpType
ACT = mybir.ActivationFunctionType
AX = mybir.AxisListType

P = 128
SEQ = 256
TB = SEQ // P
D = 1024
KD = D // P
BANK = 512
H = 8
HD = D // H // 2
FF = 2816
E = 8
FE = 3584
DP = 256
KP = DP // P
CONV = 4
EPS = 1e-6
SUB_EPS = 1e-5
LAMBDA_INIT = 0.8 - 0.6 * math.exp(-0.3 * 0)
NEG = -1e30

SLOTS = 7
SLOT = 4096
UNIT = 2048
HI_RING = 3
LO_RING = 2
CHUNK = 512
EXTRA = 3
ITEMS = E + EXTRA


def plan():
    order = [(n, 2) for n in ("k0", "k1", "q0", "q1", "v0", "v1")] + [None, ("o0", 2), ("o1", 2)]
    steps = -(-FF // CHUNK)
    for j in range(steps):
        n = 2 if (j + 1) * CHUNK <= FF else 1
        order += [(f"g{j}", n), (f"u{j}", n)]
        if j:
            order.append((f"d{j - 1}", 2))
    order.append((f"d{steps - 1}", n))
    order += [("pg0", 2), ("pg1", 2), ("pp", 1)]
    order += [("x0", 2), ("x1", 2), ("ga0", 1), ("y0", 2), None, ("ga1", 1), ("y1", 2), ("ro0", 2), ("ro1", 2)]
    return order


def moe_plan():
    steps = FE // CHUNK
    names = []
    for j in range(steps):
        names += [f"g{j}", f"u{j}"] + ([f"d{j - 1}"] if j else [])
    return names + [f"d{steps - 1}"]


def build(nc, x, p, ln_mix, ln_ffn, ln_ple, ln_final, ple_w_proj, ple_w_gate,
          attn_wq, attn_wk, attn_wv, attn_wo, attn_lambda_q1, attn_lambda_k1,
          attn_lambda_q2, attn_lambda_k2, attn_subln, ffn_w_gate, ffn_w_up, ffn_w_down,
          lru_w_in_x, lru_w_in_y, lru_conv_w, lru_conv_b, lru_gate_a_w, lru_gate_a_b,
          lru_gate_x_w, lru_gate_x_b, lru_lambda, lru_w_out,
          moe_w_router, moe_w_gate, moe_w_up, moe_w_down, rope, out):
    slot_of, unit_of, uses = {}, {}, {}
    landed_of, unit_shape = {}, {}
    count = [0] * SLOTS
    previous = {}
    owner = [None] * SLOTS
    position = n_units = 0
    dense = []
    for entry in plan():
        s = position % SLOTS
        position += 1
        if entry is None:
            continue
        name, n = entry
        slot_of[name], unit_of[name] = s, list(range(n_units, n_units + n))
        n_units += n
        count[s] += 2 if name.startswith("ga") else 1
        landed_of[name] = 16 * count[s]
        previous[name] = owner[s]
        owner[s] = name
        dense.append(name)
        for i, u in enumerate(unit_of[name]):
            unit_shape[u] = (name, i * UNIT, UNIT // 2 if name.startswith("ga") else UNIT)
    U0 = n_units
    SHIFT = position % SLOTS
    MOE = moe_plan()
    G_ITEM, U_ITEM = len(MOE), 2 * len(MOE)
    assert G_ITEM % SLOTS == 0 and U_ITEM % HI_RING == 0 and U_ITEM % LO_RING == 0
    moe_unit = {n: [2 * i, 2 * i + 1] for i, n in enumerate(MOE)}
    moe_slot = [(SHIFT + i) % SLOTS for i in range(G_ITEM)]
    LAND0 = [16 * c for c in count]
    LAND_ITEM = 16 * (G_ITEM // SLOTS)
    moe_unit_abs = {n: [U0 + u for u in us] for n, us in moe_unit.items()}
    POST = [("pg0", 2), ("pg1", 2), ("pp", 1)]
    post_unit = {"pg0": [U0, U0 + 1], "pg1": [U0 + 2, U0 + 3], "pp": [U0 + 4]}
    scatter_banks = (2, 3, 6, 7)
    tiles = [(0, 0, 4), (0, 4, 4), (1, 0, 2), (1, 2, 2), (1, 4, 2), (1, 6, 2)]

    def columns(w, n0, n):
        return w[:, n0:n0 + n].rearrange("(k p) n -> p k n", p=P)

    def rows(w, r0, n):
        return w[r0:r0 + n, :].rearrange("(k p) n -> p k n", p=P)

    source = {}
    for c in range(2):
        for n, w in (("k", attn_wk), ("q", attn_wq), ("v", attn_wv), ("o", attn_wo)):
            source[f"{n}{c}"] = columns(w[0], c * CHUNK, CHUNK)
        for n, w in (("x", lru_w_in_x), ("y", lru_w_in_y), ("ro", lru_w_out)):
            source[f"{n}{c}"] = columns(w[0], c * CHUNK, CHUNK)
        source[f"pg{c}"] = columns(ple_w_gate[0], c * CHUNK, CHUNK)
    source["pp"] = rows(ple_w_proj[0], 0, DP)
    FSTEPS = -(-FF // CHUNK)
    fwidth = [min(CHUNK, FF - j * CHUNK) for j in range(FSTEPS)]
    for j, w in enumerate(fwidth):
        source[f"g{j}"] = columns(ffn_w_gate[0], j * CHUNK, w)
        source[f"u{j}"] = columns(ffn_w_up[0], j * CHUNK, w)
        source[f"d{j}"] = rows(ffn_w_down[0], j * CHUNK, w)

    with ExitStack() as ctx:
        def sb(name, shape, dt=F32):
            return ctx.enter_context(nc.sbuf_tensor(name, shape, dt))

        def sem(name):
            return ctx.enter_context(nc.semaphore(name))

        raw = sb("raw", [P, SLOTS, SLOT])
        w_hi = sb("w_hi", [P, HI_RING, UNIT], F32R)
        w_lo = sb("w_lo", [P, LO_RING, UNIT], F32R)
        res = sb("res", [P, TB, D])
        xn = sb("xn", [P, TB, D])
        xh = sb("xh", [P, KD, SEQ], F32R)
        xl = sb("xl", [P, KD, SEQ], F32R)
        region = sb("region", [P, 2560])
        region_r = sb("region_r", [P, 2048], F32R)
        ident = sb("ident", [P, P])
        tri = sb("tri", [P, P])
        ones = sb("ones", [P, P])
        iota_row = sb("iota_row", [P, P])
        mask = sb("mask", [P, P])
        N_ROWS = 3 * 2 * KD + (CONV + 4) * KD + 1
        rows_in = sb("rows_in", [P, P])
        prm = sb("prm", [P, N_ROWS])
        gsub = sb("gsub", [P, 1])
        lam_t = sb("lam_t", [1, 8])
        nlam = sb("nlam", [P, 1])
        ss = sb("ss", [P, 8])
        ss_o = sb("ss_o", [P, 3, TB, H])
        mx = sb("mx", [P, 2, 8])
        den = sb("den", [P, 2, 8])
        rden = sb("rden", [P, 2, 8])
        lru_c = sb("lru_c", [P, 6, KD])
        rw = sb("rw", [P, KD, E])
        rw_h = sb("rw_h", [P, KD, E], F32R)
        rw_l = sb("rw_l", [P, KD, E], F32R)
        small = sb("small", [P, 16, TB])
        rev = sb("rev", [P, TB, E])
        item_pos = sb("item_pos", [P, TB, ITEMS + 2])
        item_gate = sb("item_gate", [P, TB, ITEMS + 2])
        over = sb("over", [P, 6, E])
        ctl_f = sb("ctl_f", [P, EXTRA + 1])
        ctl = sb("ctl", [P, EXTRA + 1], I32)
        cur = sb("cur", [P, 2 * TB])
        ps = ctx.enter_context(nc.psum_tensor("ps", [P, 8, BANK], F32))

        def col(which, k):
            return prm[:, which * KD + k:which * KD + k + 1]
        MIX, FFN, PLE, CW, CB, BA, BX, LAM = 0, 2, 4, 6, 10, 11, 12, 13
        SUB = prm[:, N_ROWS - 1:N_ROWS]

        rot_a, rot_b = xn[:, 0, 0:BANK], xn[:, 0, BANK:D]
        rot = xn[:, 1, :].rearrange("p (t n) -> p t n", t=TB)
        qT = raw[:, SLOTS - 1, 0:KD * SEQ].rearrange("p (k t) -> p k t", k=KD)
        kT = raw[:, SLOTS - 1, KD * SEQ:2 * KD * SEQ].rearrange("p (k t) -> p k t", k=KD)
        v_sb = region[:, 0:TB * D].rearrange("p (t n) -> p t n", t=TB)
        wT = region[:, TB * D:TB * D + BANK]
        sc_sb = xn[:, 1, :].rearrange("p (m n) -> p m n", m=2)
        lam_in = region[0:1, 0:4 * HD].rearrange("p (i n) -> p i n", i=4)
        cosb = region[:, 256:384].rearrange("p (t a f) -> p t a f", t=TB, a=2)
        nsin = region[:, 384:448].rearrange("p (t f) -> p t f", t=TB)
        route = region[:, 2304:2432].rearrange("p (i t e) -> p i t e", i=8, t=TB)
        hid = region[:, 0:TB * CHUNK].rearrange("p (t n) -> p t n", t=TB)
        hTh = region_r[:, 0:1024].rearrange("p (k t) -> p k t", k=4)
        hTl = region_r[:, 1024:2048].rearrange("p (k t) -> p k t", k=4)
        p_in = region[:, 0:TB * DP].rearrange("p (t n) -> p t n", t=TB)
        sig = region[:, 512:512 + TB * BANK].rearrange("p (t n) -> p t n", t=TB)
        pTh = region_r[:, 0:KP * SEQ].rearrange("p (k t) -> p k t", k=KP)
        pTl = region_r[:, 1024:1024 + KP * SEQ].rearrange("p (k t) -> p k t", k=KP)
        XPW = SEQ + CONV - 1
        xp = region[:, 0:4 * XPW].rearrange("p (c t) -> p c t", c=4)
        four = lambda a: a.rearrange("p (c t) -> p c t", c=4)
        u_half = [four(region[:, 1152:2176]), four(raw[:, SLOTS - 1, 2048:3072])]
        sq_half = four(raw[:, SLOTS - 1, 3072:4096])
        uh, ul = four(region_r[:, 0:1024]), four(region_r[:, 1024:2048])
        lru_r, lru_i = four(xn[:, 0, :]), four(xn[:, 1, :])
        lru_h = raw[:, SLOTS - 1, 0:2048].rearrange("p (k t) -> p k t", k=KD)
        lru_y = raw[:, SLOTS - 1, 2048:4096].rearrange("p (k t) -> p k t", k=KD)
        sel = region[:, 0:256].rearrange("p (t s) -> p t s", t=TB)
        sel_g = region[:, 256:512].rearrange("p (t s) -> p t s", t=TB)
        sel_gT = region[:, 512:768]
        m_hid = region[:, 768:1280]
        y_sb = region[:, 1280:2304]
        mTh = region_r[:, 0:512].rearrange("p (k t) -> p k t", k=4)
        mTl = region_r[:, 512:1024].rearrange("p (k t) -> p k t", k=4)
        lnf_row = region[:, 1536:2560]

        landed = [sem(f"landed{s}") for s in range(SLOTS)]
        hi_done, lo_done, unit_used = sem("hi_done"), sem("lo_done"), sem("unit_used")
        x_in, rows_landed, rope_in, lam_landed, rw_in, p_landed, lnf_in, stored = map(sem, (
            "x_in", "rows_landed", "rope_in", "lam_landed", "rw_in", "p_landed", "lnf_in", "stored"))
        zeroed, consts = sem("zeroed"), sem("consts")
        prm_psum, prm_ready = sem("prm_psum"), sem("prm_ready")
        lam_summed, lam_exp, lam_ready, lam_psum = map(sem, ("lam_summed", "lam_exp", "lam_ready", "lam_psum"))
        lru_exp, lru_ready = sem("lru_exp"), sem("lru_ready")
        dve_chain = sem("dve_chain")
        squared, mean_ready, root_ready, xn_ready = map(sem, ("squared", "mean_ready", "root_ready", "xn_ready"))
        xT_psum, xh_ready, xl_ready = map(sem, ("xT_psum", "xh_ready", "xl_ready"))
        rope_read, rot_ready, rot_psum, qk_ready, v_ready = map(sem, (
            "rope_read", "rot_ready", "rot_psum", "qk_ready", "v_ready"))
        scored, masked, max_ready, exp_ready, weighed, wT_psum, wT_ready, pv_done = map(sem, (
            "scored", "masked", "max_ready", "exp_ready", "weighed", "wT_psum", "wT_ready", "pv_done"))
        o_squared, o_copied, o_mean, o_root, o_ready, oT_psum, oh_ready, ol_ready, res_added = map(sem, (
            "o_squared", "o_copied", "o_mean", "o_root", "o_ready", "oT_psum", "oh_ready", "ol_ready", "res_added"))
        silu_done, hid_ready, hT_psum, hTh_ready, hTl_ready = map(sem, (
            "silu_done", "hid_ready", "hT_psum", "hTh_ready", "hTl_ready"))
        pT_psum, pTh_ready, pTl_ready, gate_ready = map(sem, (
            "pT_psum", "pTh_ready", "pTl_ready", "gate_ready"))
        xp_zero, xp_ready, tap_ready, conv_ready, uh_ready, ul_ready = map(sem, (
            "xp_zero", "xp_ready", "tap_ready", "conv_ready", "uh_ready", "ul_ready"))
        sig_ready, tanh_ready, sqrt_ready, scan_read, scan_ready, gelu_ready, z_ready, zh_ready, zl_ready = map(sem, (
            "sig_ready", "tanh_ready", "sqrt_ready", "scan_read", "scan_ready", "gelu_ready", "z_ready", "zh_ready", "zl_ready"))
        rw_h_ready, rw_l_ready, logits_ready, gap_ready, gap_exp, chosen, ranked, items_ready = map(sem, (
            "rw_h_ready", "rw_l_ready", "logits_ready", "gap_ready", "gap_exp", "chosen", "ranked", "items_ready"))
        cur_ready, sel_ready, selT_psum, selT_ready, gathered, gh_ready, gl_ready, y_act, y_dve, scattered = map(sem, (
            "cur_ready", "sel_ready", "selT_psum", "selT_ready", "gathered", "gh_ready", "gl_ready",
            "y_act", "y_dve", "scattered"))
        final_ready = sem("final_ready")

        block = ctx.enter_context(nc.Block())

        @block.sync
        def _(sp):
            def load_dense(name):
                if previous[name]:
                    sp.wait_ge(lo_done, unit_of[previous[name]][-1] + 1)
                if name == "d0":
                    sp.wait_ge(scored, 6)
                s = slot_of[name]
                if name.startswith("ga"):
                    c = int(name[2])
                    for i, w in enumerate((lru_gate_a_w, lru_gate_x_w)):
                        dst = raw[:, s, i * BANK:(i + 1) * BANK].rearrange("p (n d) -> p n d", n=4)
                        sp.dma_start(dst, w[0, 4 * c:4 * c + 4].rearrange("n c d -> c n d")).then_inc(landed[s], 16)
                    return
                src = source[name]
                dst = raw[:, s, 0:src.shape[1] * src.shape[2]].rearrange("p (k n) -> p k n", k=src.shape[1])
                sp.dma_start(dst, src).then_inc(landed[s], 16)

            def load_item(it, e):
                for i, name in enumerate(MOE):
                    s = moe_slot[i]
                    if i >= SLOTS:
                        sp.wait_ge(lo_done, U_ITEM * it + (U0 + 2 * (i - SLOTS + 1)))
                    elif not isinstance(it, int):
                        sp.wait_ge(lo_done, U_ITEM * it + (U0 - U_ITEM + 2 * (i + G_ITEM - SLOTS + 1)))
                    elif owner[s]:
                        sp.wait_ge(lo_done, unit_of[owner[s]][-1] + 1)
                        if s == SLOTS - 1:
                            sp.wait_ge(zl_ready, 2)
                    j = int(name[1:])
                    one = bass.ds(e, 1)
                    if name[0] == "d":
                        src = moe_w_down[0][one, j * CHUNK:(j + 1) * CHUNK, :].rearrange("e (k p) n -> p (e k) n", p=P)
                        dst = raw[:, s, :].rearrange("p (k n) -> p k n", n=D)
                    else:
                        w = moe_w_gate if name[0] == "g" else moe_w_up
                        src = w[0][one, :, j * CHUNK:(j + 1) * CHUNK].rearrange("e (k p) n -> p (e k) n", p=P)
                        dst = raw[:, s, :].rearrange("p (k n) -> p k n", n=CHUNK)
                    sp.dma_start(dst, src).then_inc(landed[s], 16)

            sp.dma_start(res[:], x[0].rearrange("(t p) d -> p t d", p=P)).then_inc(x_in, 16)
            for name in dense:
                load_dense(name)
            load_item(0, 0)
            with sp.Fori(1, E) as it:
                load_item(it, it)
            sp.wait_ge(items_ready, 1)
            extra = sp.value_load(ctl[0:1, EXTRA:EXTRA + 1], min_val=0, max_val=EXTRA)
            with sp.If(extra > 0):
                with sp.Fori(0, extra) as i:
                    e = sp.value_load(ctl[0:1, bass.ds(i, 1)], min_val=0, max_val=E - 1)
                    load_item(i + E, e)
            items = sp.snap(extra + E)
            for i, (name, n) in enumerate(POST):
                s = (SHIFT + i) % SLOTS
                sp.wait_ge(lo_done, U_ITEM * items + (U0 - U_ITEM + 2 * (i + G_ITEM - SLOTS + 1)))
                if name == "pp":
                    src = rows(ple_w_proj[1], 0, DP)
                else:
                    src = columns(ple_w_gate[1], int(name[2]) * CHUNK, CHUNK)
                dst = raw[:, s, 0:src.shape[1] * src.shape[2]].rearrange("p (k n) -> p k n", k=src.shape[1])
                sp.dma_start(dst, src).then_inc(landed[s], 16)
            for t in range(TB):
                sp.wait_ge(final_ready, t + 1)
                sp.dma_start(out[0].rearrange("(t p) d -> p t d", p=P)[:, t, :], xn[:, t, :]).then_inc(stored, 16)
            sp.wait_ge(stored, 16 * TB)

        @block.gpsimd
        def _(pool):
            pool.memset(ident[:], 0.0).then_inc(zeroed, 1)
            pool.memset(mask[:], 0.0).then_inc(zeroed, 1)
            pool.memset(tri[:], 1.0).then_inc(zeroed, 1)
            pool.memset(ones[:], 1.0).then_inc(consts, 1)
            pool.wait_ge(zeroed, 3)
            pool.affine_select(out=ident[:], in_=ident[:], compare_op=ALU.not_equal, fill=1.0, base=0,
                               pattern=[[-1, P]], channel_multiplier=1).then_inc(consts, 1)
            pool.affine_select(out=mask[:], in_=mask[:], compare_op=ALU.is_ge, fill=NEG, base=0,
                               pattern=[[-1, P]], channel_multiplier=1).then_inc(consts, 1)
            pool.affine_select(out=tri[:], in_=tri[:], compare_op=ALU.is_ge, fill=0.0, base=-1,
                               pattern=[[1, P]], channel_multiplier=-1).then_inc(consts, 1)
            pool.iota(iota_row[:], [[1, P]], base=0, channel_multiplier=0,
                      allow_small_or_imprecise_dtypes=True).then_inc(consts, 1)
            pool.iota(rev[:], [[0, TB], [-1, E]], base=E, channel_multiplier=0,
                      allow_small_or_imprecise_dtypes=True).then_inc(consts, 1)
            at = 0
            for w, n in ((ln_mix, 2 * KD), (ln_ffn, 2 * KD), (ln_ple, 2 * KD)):
                pool.dma_start(rows_in[at:at + n, :], w.rearrange("l (k p) -> (l k) p", p=P)).then_inc(rows_landed, 16)
                at += n
            pool.dma_start(rows_in[at:at + CONV * KD, :],
                           lru_conv_w[0].rearrange("i (k p) -> (i k) p", p=P)).then_inc(rows_landed, 16)
            at += CONV * KD
            for w in (lru_conv_b, lru_gate_a_b, lru_gate_x_b, lru_lambda):
                pool.dma_start(rows_in[at:at + KD, :], w.rearrange("l (k p) -> (l k) p", p=P)).then_inc(rows_landed, 16)
                at += KD
            pool.dma_start(rows_in[at:at + 1, :], attn_subln).then_inc(rows_landed, 16)
            pool.dma_start(cosb[:], rope[:, 0:2, :].rearrange("(t p) a f -> p t a f", p=P)).then_inc(rope_in, 16)
            pool.dma_start(nsin[:], rope[:, 2, :].rearrange("(t p) f -> p t f", p=P)).then_inc(rope_in, 16)
            for i, w in enumerate((attn_lambda_q1, attn_lambda_q2, attn_lambda_k1, attn_lambda_k2)):
                pool.dma_start(lam_in[:, i, :], w).then_inc(lam_landed, 16)
            pool.dma_start(rw[:], moe_w_router[0].rearrange("(k p) e -> p k e", p=P)).then_inc(rw_in, 16)
            pool.wait_ge(res_added, 12)
            pool.memset(xp[:, :, 0:CONV - 1], 0.0).then_inc(xp_zero, 1)

        @block.tensor
        def _(pe):
            def bank(b, c0=0, n=BANK):
                return ps[:, b, c0:c0 + n]

            def hi(u, off, n):
                return w_hi[:, (u % HI_RING), off:off + n]

            def lo(u, off, n):
                return w_lo[:, (u % LO_RING), off:off + n]

            def project(us, base, kind, width, a_hi, a_lo, tbs, banks, k_total, first=True, last=True):
                per = k_total // len(us)
                for i, u in enumerate(us):
                    pieces = []
                    for kk in range(per):
                        k = i * per + kk
                        if kind == "columns":
                            pieces.append((k, 0, kk * width, width))
                        else:
                            pieces += [(k, n, kk * D + n * BANK, BANK) for n in range(2)]
                    pe.wait_ge(hi_done, base + (u + 1))
                    for t in range(tbs):
                        for k, n, off, w in pieces:
                            b = bank(banks[t][n], 0, w)
                            pe.matmul(b, a_hi[:, k, t * P:(t + 1) * P], hi(u, off, w), start=(first and k == 0), stop=False,
                                      skip_group_check=True)
                            pe.matmul(b, a_lo[:, k, t * P:(t + 1) * P], hi(u, off, w), start=False, stop=False,
                                      skip_group_check=True)
                    pe.wait_ge(lo_done, base + (u + 1))
                    for t in range(tbs):
                        for k, n, off, w in pieces:
                            mm = pe.matmul(bank(banks[t][n], 0, w), a_hi[:, k, t * P:(t + 1) * P], lo(u, off, w),
                                           start=False, stop=(last and k == k_total - 1), skip_group_check=True)
                    mm.then_inc(unit_used, 1)

            def norm_transposes(n_done):
                for t in range(TB):
                    pe.wait_ge(xn_ready, n_done * TB + t + 1)
                    for k in range(KD):
                        tr = pe.transpose(ps[:, k // 2, (k % 2) * SEQ + t * P:(k % 2) * SEQ + (t + 1) * P],
                                          xn[:, t, k * P:(k + 1) * P], ident[:])
                        if t == TB - 1 and k % 2:
                            tr.then_inc(xT_psum, 1)

            def gated_ffn(steps, us_of, base, a_hi, a_lo, th, tl, hid_at, tbs, k_of, pairs, acc, done, width):
                for j in range(steps):
                    w = width[j]
                    g_banks = [[pairs[j % 2][t]] for t in range(tbs)]
                    u_banks = [[pairs[1 - j % 2][t]] for t in range(tbs)]
                    if j or not isinstance(done, int) or done:
                        pe.wait_ge(hid_ready, tbs * j + done)
                    project(us_of[f"g{j}"], base, "columns", w, a_hi, a_lo, tbs, g_banks, KD)
                    if j or not isinstance(done, int) or done:
                        pe.wait_ge(hTh_ready, tbs * j + done)
                        pe.wait_ge(hTl_ready, tbs * j + done)
                    project(us_of[f"u{j}"], base, "columns", w, a_hi, a_lo, tbs, u_banks, KD)
                    if j:
                        down(j - 1, us_of, base, th, tl, tbs, acc, steps, width)
                    for t in range(tbs):
                        pe.wait_ge(hid_ready, tbs * j + (t + 1) + done)
                        for c in range(w // P):
                            tr = pe.transpose(bank(g_banks[t][0], c * P, P), hid_at(t)[:, c * P:(c + 1) * P], ident[:])
                        tr.then_inc(hT_psum, 1)

            def down(j, us_of, base, th, tl, tbs, acc, steps, width):
                project(us_of[f"d{j}"], base, "rows", D, th, tl, tbs, acc, width[j] // P,
                        first=(j == 0), last=(j == steps - 1))

            def transposed_project(name, banks, first_bank_wait=None):
                for i, u in enumerate(unit_of[name]):
                    pe.wait_ge(hi_done, u + 1)
                    for c in range(4):
                        for kk in range(4):
                            k = 4 * i + kk
                            w = hi(u, kk * CHUNK + c * P, P)
                            pe.matmul(bank(banks[c], 0, SEQ), w, xh[:, k, :], start=(k == 0), stop=False,
                                      skip_group_check=True)
                            pe.matmul(bank(banks[c], 0, SEQ), w, xl[:, k, :], start=False, stop=False,
                                      skip_group_check=True)
                    pe.wait_ge(lo_done, u + 1)
                    for c in range(4):
                        for kk in range(4):
                            k = 4 * i + kk
                            mm = pe.matmul(bank(banks[c], 0, SEQ), lo(u, kk * CHUNK + c * P, P), xh[:, k, :],
                                           start=False, stop=(k == KD - 1), skip_group_check=True)
                    mm.then_inc(unit_used, 1)

            def embedding(layer, us_of, base, norms):
                pe.wait_ge(p_landed, 16 * (layer + 1))
                for k in range(KP):
                    for t in range(TB):
                        tr = pe.transpose(bank(4, k * SEQ + t * P, P), p_in[:, t, k * P:(k + 1) * P], ident[:])
                tr.then_inc(pT_psum, 1)
                norm_transposes(norms)
                pe.wait_ge(xh_ready, 4 * (norms + 1))
                pe.wait_ge(xl_ready, 4 * (norms + 1))
                pe.wait_ge(pTh_ready, layer + 1)
                pe.wait_ge(pTl_ready, layer + 1)
                for c in range(2):
                    project(us_of[f"pg{c}"], base, "columns", BANK, xh, xl, TB, [[4 + 2 * c], [5 + 2 * c]], KD)
                project(us_of["pp"], base, "rows", D, pTh, pTl, TB, [[0, 1], [2, 3]], KP)

            pe.wait_ge(consts, 6)
            pe.wait_ge(rows_landed, 16 * 9)
            pe.transpose(bank(7, 0, N_ROWS), rows_in[0:N_ROWS, :], ident[0:N_ROWS, 0:N_ROWS]).then_inc(prm_psum, 1)
            pe.wait_ge(lam_ready, 1)
            pe.matmul(bank(6, 0, 1), ones[0:1, :], lam_t[0:1, 4:5], start=True, stop=True).then_inc(lam_psum, 1)

            norm_transposes(0)
            pe.wait_ge(xh_ready, 4)
            pe.wait_ge(xl_ready, 4)

            def rot_transposes(n, banks):
                pe.wait_ge(rot_ready, TB * (n + 1))
                for t in range(TB):
                    for c in range(4):
                        tr = pe.transpose(bank(banks[c // 2], (c % 2) * SEQ + t * P, P), rot[:, t, c * P:(c + 1) * P], ident[:])
                tr.then_inc(rot_psum, 1)

            def attn_project(name, banks):
                project(unit_of[name], 0, "columns", BANK, xh, xl, TB, [[banks[0]], [banks[1]]], KD)

            attn_project("k0", (4, 5))
            attn_project("k1", (6, 7))
            rot_transposes(0, (4, 5))
            attn_project("q0", (0, 1))
            rot_transposes(1, (6, 7))
            attn_project("q1", (2, 3))
            rot_transposes(2, (0, 1))
            pe.wait_ge(qk_ready, 1)
            attn_project("v0", (4, 5))
            rot_transposes(3, (2, 3))
            pe.wait_ge(qk_ready, 2)
            attn_project("v1", (6, 7))

            def scores(n):
                qb, h0, nh = tiles[n]
                keys = (qb + 1) * P
                if n == 0:
                    pe.wait_ge(qk_ready, 4)
                if n >= 2:
                    pe.wait_ge(masked, n - 1)
                for m in range(2):
                    for i in range(nh):
                        mm = pe.matmul(bank(2 * (n % 2) + m, i * keys, keys),
                                       qT[m * HD:(m + 1) * HD, h0 + i, qb * P:(qb + 1) * P],
                                       kT[m * HD:(m + 1) * HD, h0 + i, 0:keys], start=True, stop=True)
                mm.then_inc(scored, 1)

            def weights_times_values(n):
                qb, h0, nh = tiles[n]
                pe.wait_ge(weighed, n + 1)
                if n == 0:
                    pe.wait_ge(v_ready, 2)
                for i in range(nh):
                    for kb in range(qb + 1):
                        c = i * (qb + 1) + kb
                        tr = pe.transpose(bank(4 + n % 2, c * P, P), sc_sb[:, 0, c * P:(c + 1) * P], ident[:])
                tr.then_inc(wT_psum, 1)
                pe.wait_ge(wT_ready, n + 1)
                if n == 2:
                    pe.wait_ge(o_copied, 1)
                    pe.wait_ge(o_squared, 1)
                for i in range(nh):
                    h = h0 + i
                    for kb in range(qb + 1):
                        c = i * (qb + 1) + kb
                        mm = pe.matmul(bank(6 + h // 4, (h % 4) * P, P), wT[:, c * P:(c + 1) * P],
                                       v_sb[:, kb, h * P:(h + 1) * P], start=(kb == 0), stop=(kb == qb))
                mm.then_inc(pv_done, 1)

            scores(0)
            for n in range(len(tiles)):
                if n + 1 < len(tiles):
                    scores(n + 1)
                weights_times_values(n)
            pe.wait_ge(masked, len(tiles))
            for t in range(TB):
                pe.wait_ge(o_ready, t + 1)
                for k in range(KD):
                    tr = pe.transpose(ps[:, k // 2, (k % 2) * SEQ + t * P:(k % 2) * SEQ + (t + 1) * P],
                                      xn[:, t, k * P:(k + 1) * P], ident[:])
                    if t == TB - 1 and k % 2:
                        tr.then_inc(oT_psum, 1)
            pe.wait_ge(oh_ready, 4)
            pe.wait_ge(ol_ready, 4)
            attn_project("o0", (4, 5))
            pe.wait_ge(o_copied, 2)
            pe.wait_ge(o_squared, 2)
            attn_project("o1", (6, 7))

            norm_transposes(1)
            pe.wait_ge(xh_ready, 8)
            pe.wait_ge(xl_ready, 8)
            pe.wait_ge(res_added, 4)
            dense_acc = [[4, 5], [6, 7]]
            gated_ffn(FSTEPS, unit_of, 0, xh, xl, hTh, hTl, lambda t: hid[:, t, :], TB, None,
                      ((0, 1), (2, 3)), dense_acc, 0, fwidth)
            pe.wait_ge(hTh_ready, TB * FSTEPS)
            pe.wait_ge(hTl_ready, TB * FSTEPS)
            down(FSTEPS - 1, unit_of, 0, hTh, hTl, TB, dense_acc, FSTEPS, fwidth)

            pe.wait_ge(res_added, 8)
            embedding(0, unit_of, 0, 2)

            pe.wait_ge(res_added, 12)
            norm_transposes(3)
            pe.wait_ge(xh_ready, 16)
            pe.wait_ge(xl_ready, 16)
            transposed_project("x0", (4, 5, 6, 7))
            transposed_project("x1", (0, 1, 2, 3))

            def lru_gates(c):
                u = unit_of[f"ga{c}"][0]
                pe.wait_ge(uh_ready, c + 1)
                pe.wait_ge(hi_done, u + 1)
                pe.wait_ge(ul_ready, c + 1)
                pe.wait_ge(lo_done, u + 1)
                if c:
                    pe.wait_ge(sig_ready, 1)
                for b in range(4):
                    for g in range(2):
                        o = bank(4 + b, g * SEQ, SEQ)
                        w = g * BANK + b * P
                        pe.matmul(o, hi(u, w, P), uh[:, b, :], start=True, stop=False)
                        pe.matmul(o, hi(u, w, P), ul[:, b, :], start=False, stop=False)
                        mm = pe.matmul(o, lo(u, w, P), uh[:, b, :], start=False, stop=True)
                mm.then_inc(unit_used, 1)

            lru_gates(0)
            pe.wait_ge(xp_ready, 2)
            pe.wait_ge(tap_ready, 8)
            transposed_project("y0", (0, 1, 2, 3))
            lru_gates(1)
            pe.wait_ge(sig_ready, 2)
            transposed_project("y1", (4, 5, 6, 7))
            pe.wait_ge(zh_ready, 2)
            pe.wait_ge(zl_ready, 2)
            pe.wait_ge(gelu_ready, 2)
            for c in range(2):
                project(unit_of[f"ro{c}"], 0, "columns", BANK, xh, xl, TB, [[2 * c], [2 * c + 1]], KD)

            pe.wait_ge(res_added, 16)
            norm_transposes(4)
            pe.wait_ge(xh_ready, 20)
            pe.wait_ge(xl_ready, 20)
            pe.wait_ge(rw_h_ready, 1)
            pe.wait_ge(rw_l_ready, 1)
            for t in range(TB):
                for k in range(KD):
                    for i, (a, w) in enumerate(((xh, rw_h), (xl, rw_h), (xh, rw_l))):
                        mm = pe.matmul(bank(4 + t, 0, E), a[:, k, t * P:(t + 1) * P], w[:, k, :],
                                       start=(k == 0 and i == 0), stop=(k == KD - 1 and i == 2))
            mm.then_inc(logits_ready, 1)
            chose = route[:, 4]
            pe.wait_ge(chosen, 1)
            pe.matmul(bank(6, 0, E), tri[:], chose[:, 0, :], start=True, stop=True)
            pe.matmul(bank(7, 0, E), ones[:], chose[:, 0, :], start=True, stop=False)
            pe.matmul(bank(7, 0, E), tri[:], chose[:, 1, :], start=False, stop=True)
            pe.matmul(bank(5, 0, E), ones[:], chose[:, 0, :], start=True, stop=False)
            pe.matmul(bank(5, 0, E), ones[:], chose[:, 1, :], start=False, stop=True).then_inc(ranked, 1)

            def gather(n):
                pe.wait_ge(sel_ready, n + 1)
                for k in range(KD):
                    for t in range(TB):
                        mm = pe.matmul(bank(6 + k // 4, (k % 4) * P, P), xn[:, t, k * P:(k + 1) * P], sel[:, t, :],
                                       start=(t == 0), stop=(t == TB - 1))
                mm.then_inc(gathered, 1)

            gather(0)
            pe.wait_ge(items_ready, 1)
            extra = pe.value_load(ctl[0:1, EXTRA:EXTRA + 1], min_val=0, max_val=EXTRA)
            items = pe.snap(extra + E)
            STEPS = FE // CHUNK
            moe_acc = [[4, 5]]
            dense_hid = TB * FSTEPS
            with pe.Fori(0, items) as it:
                for t in range(TB):
                    tr = pe.transpose(bank(2, t * P, P), sel_g[:, t, :], ident[:])
                tr.then_inc(selT_psum, 1)
                pe.wait_ge(gh_ready, it + 1)
                pe.wait_ge(gl_ready, it + 1)
                done = STEPS * it + dense_hid
                gated_ffn(STEPS, moe_unit_abs, U_ITEM * it, xh, xl, mTh, mTl, lambda t: m_hid, 1, None,
                          ((0,), (1,)), moe_acc, done, [CHUNK] * STEPS)
                gather(it + 1)
                pe.wait_ge(hTh_ready, done + STEPS)
                pe.wait_ge(hTl_ready, done + STEPS)
                down(STEPS - 1, moe_unit_abs, U_ITEM * it, mTh, mTl, 1, moe_acc, STEPS, [CHUNK] * STEPS)
                pe.wait_ge(y_act, it + 1)
                pe.wait_ge(y_dve, it + 1)
                pe.wait_ge(selT_ready, it + 1)
                pe.wait_ge(gh_ready, it + 2)
                pe.wait_ge(gl_ready, it + 2)
                for t in range(TB):
                    for n in range(2):
                        mm = pe.matmul(bank(scatter_banks[2 * t + n]), sel_gT[:, t * P:(t + 1) * P],
                                       y_sb[:, n * BANK:(n + 1) * BANK], start=True, stop=True)
                mm.then_inc(scattered, 1)
                pe.wait_ge(res_added, 4 * it + 20)

            embedding(1, post_unit, U_ITEM * items, 5)

        @block.scalar
        def _(act):
            class split:
                at = 0

            def split_dense(upto):
                while split.at < min(upto, U0):
                    u = split.at
                    split.at += 1
                    name, off, n = unit_shape[u]
                    s = slot_of[name]
                    act.wait_ge(landed[s], landed_of[name])
                    if u >= HI_RING:
                        act.wait_ge(unit_used, u - HI_RING + 1)
                    act.activation(w_hi[:, u % HI_RING, 0:n], raw[:, s, off:off + n], ACT.Copy).then_inc(hi_done, 1)

            def split_moe(it, first, upto):
                for u in range(first, min(upto, U_ITEM)):
                    g = u // 2
                    s = moe_slot[g]
                    turn = sum(x == s for x in moe_slot[:g + 1])
                    act.wait_ge(landed[s], LAND_ITEM * it + (LAND0[s] + 16 * turn))
                    act.wait_ge(unit_used, U_ITEM * it + (U0 + u - HI_RING + 1))
                    off = (u % 2) * UNIT
                    act.activation(w_hi[:, (U0 + u) % HI_RING, :], raw[:, s, off:off + UNIT], ACT.Copy).then_inc(hi_done, 1)

            def squares(src_ready=None):
                for t in range(TB):
                    act.activation(xn[:, t, :], res[:, t, :], ACT.Square, accum_out=ss[:, t:t + 1]).then_inc(squared, 1)

            def norm(n, gain):
                squares()
                act.wait_ge(mean_ready, n + 1)
                act.activation(ss[:, 4:6], ss[:, 2:4], ACT.Sqrt).then_inc(root_ready, 1)

            def norm_hi(n, gain):
                for k in range(KD):
                    if k % 2 == 0:
                        act.wait_ge(xT_psum, 4 * n + k // 2 + 1)
                    a = act.activation(xh[:, k, :], ps[:, k // 2, (k % 2) * SEQ:(k % 2 + 1) * SEQ], ACT.Copy,
                                       scale=col(gain, k))
                    if k % 2:
                        a.then_inc(xh_ready, 1)

            act.wait_ge(x_in, 16)
            squares()
            act.wait_ge(mean_ready, 1)
            act.activation(ss[:, 4:6], ss[:, 2:4], ACT.Sqrt).then_inc(root_ready, 1)
            act.wait_ge(lam_summed, 1)
            act.activation(lam_t[:, 2:4], lam_t[:, 0:2], ACT.Exp).then_inc(lam_exp, 1)
            act.wait_ge(prm_ready, 1)
            act.wait_ge(lru_exp, 1)
            act.activation(lru_c[:, 1, :], lru_c[:, 0, :], ACT.Exp, scale=-1.0).then_inc(lru_exp, 1)
            split_dense(HI_RING)
            norm_hi(0, MIX)

            used = lambda name: unit_of[name][-1] + 1
            split_dense(used("k1") + 2)

            def copy_turned(n, banks, dst, c):
                act.wait_ge(rot_psum, n + 1)
                for b in range(2):
                    a = act.activation(dst[:, 4 * c + 2 * b:4 * c + 2 * b + 2, :],
                                       ps[:, banks[b], :].rearrange("p (k t) -> p k t", k=2), ACT.Copy)
                a.then_inc(qk_ready, 1)

            copy_turned(0, (4, 5), kT, 0)
            split_dense(used("q0") + 2)
            copy_turned(1, (6, 7), kT, 1)
            split_dense(used("q1") + 2)
            copy_turned(2, (0, 1), qT, 0)
            split_dense(used("v0") + 2)
            copy_turned(3, (2, 3), qT, 1)
            act.wait_ge(unit_used, used("v0"))
            for t in range(TB):
                a = act.activation(v_sb[:, t, 0:BANK], ps[:, 4 + t, :], ACT.Copy)
            a.then_inc(v_ready, 1)
            split_dense(used("v1") + 2)
            act.wait_ge(unit_used, used("v1"))
            for t in range(TB):
                a = act.activation(v_sb[:, t, BANK:D], ps[:, 6 + t, :], ACT.Copy)
            a.then_inc(v_ready, 1)

            for n, (qb, h0, nh) in enumerate(tiles):
                keys = (qb + 1) * P
                act.wait_ge(max_ready, n + 1)
                for m in range(2):
                    for i in range(nh):
                        a = act.activation(sc_sb[:, m, i * keys:(i + 1) * keys], sc_sb[:, m, i * keys:(i + 1) * keys],
                                           ACT.Exp, scale=HD ** -0.5, bias=mx[:, m, i:i + 1],
                                           accum_out=den[:, m, i:i + 1])
                a.then_inc(exp_ready, 1)
                act.wait_ge(wT_psum, n + 1)
                act.activation(wT, ps[:, 4 + n % 2, :], ACT.Copy).then_inc(wT_ready, 1)
                if n == 1 or n == len(tiles) - 1:
                    act.wait_ge(o_copied, qb + 1)
                    for h in range(H):
                        a = act.activation(ps[:, 6 + h // 4, (h % 4) * P:(h % 4 + 1) * P], xn[:, qb, h * P:(h + 1) * P], ACT.Square,
                                           accum_out=ss_o[:, 2, qb, h:h + 1])
                    a.then_inc(o_squared, 1)
            act.wait_ge(o_mean, 1)
            act.activation(ss_o[:, 1], ss_o[:, 0], ACT.Sqrt).then_inc(o_root, 1)
            for k in range(4):
                act.wait_ge(oT_psum, k + 1)
                act.activation(xh[:, 2 * k:2 * k + 2, :], ps[:, k, :].rearrange("p (k t) -> p k t", k=2), ACT.Copy,
                               scale=gsub[:, 0:1]).then_inc(oh_ready, 1)
            split_dense(used("o1") + 2)

            def normalise(n, gain, added):
                act.wait_ge(res_added, added)
                squares()
                act.wait_ge(mean_ready, n + 1)
                act.activation(ss[:, 4:6], ss[:, 2:4], ACT.Sqrt).then_inc(root_ready, 1)
                norm_hi(n, gain)

            normalise(1, FFN, 4)
            for j in range(FSTEPS):
                w = fwidth[j]
                split_dense(used(f"g{j}") + 2)
                act.wait_ge(unit_used, used(f"g{j}"))
                if j:
                    act.wait_ge(hT_psum, TB * j)
                for t in range(TB):
                    act.activation(hid[:, t, 0:w], ps[:, 2 * (j % 2) + t, 0:w], ACT.Silu).then_inc(silu_done, 1)
                split_dense((used(f"d{j - 1}") if j else used("u0")) + 2)
                for t in range(TB):
                    act.wait_ge(hT_psum, TB * j + t + 1)
                    act.activation(hTh[:, 0:w // P, t * P:(t + 1) * P],
                                   ps[:, 2 * (j % 2) + t, 0:w].rearrange("p (k t) -> p k t", t=P),
                                   ACT.Copy).then_inc(hTh_ready, 1)
            act.dma_start(p_in, p[0, 0].rearrange("(t p) d -> p t d", p=P)).then_inc(p_landed, 16)
            split_dense(used(f"d{FSTEPS - 1}") + 2)

            def embedding_hi(layer, n, added):
                act.wait_ge(pT_psum, layer + 1)
                act.activation(pTh, ps[:, 4, :].rearrange("p (k t) -> p k t", k=KP), ACT.Copy).then_inc(pTh_ready, 1)
                normalise(n, PLE + layer, added)

            def embedding_gate(c, used_to, added):
                act.wait_ge(unit_used, used_to)
                if c:
                    act.wait_ge(res_added, added + TB)
                for t in range(TB):
                    act.activation(sig[:, t, :], ps[:, 4 + 2 * c + t, :], ACT.Sigmoid).then_inc(gate_ready, 1)

            embedding_hi(0, 2, 8)
            split_dense(used("pg0") + 2)
            embedding_gate(0, used("pg0"), 8)
            split_dense(used("pg1") + 2)
            split_dense(used("pp") + 2)
            embedding_gate(1, used("pg1"), 8)

            normalise(3, MIX + 1, 12)

            def conv_in(c, name):
                act.wait_ge(unit_used, used(name))
                if c == 0:
                    act.wait_ge(xp_zero, 1)
                else:
                    act.wait_ge(conv_ready, 1)
                b0 = 4 - 4 * c
                for b in range(4):
                    k = 4 * c + b
                    act.activation(u_half[c][:, b, :], ps[:, b0 + b, 0:SEQ], ACT.Identity, scale=col(CW + CONV - 1, k),
                                   bias=col(CB, k)).then_inc(tap_ready, 1)
                act.activation(xp[:, :, CONV - 1:], ps[:, b0:b0 + 4, 0:SEQ], ACT.Copy).then_inc(xp_ready, 1)

            def conv_out(c):
                act.wait_ge(conv_ready, c + 1)
                if c:
                    act.wait_ge(unit_used, used("ga0"))
                act.activation(uh, u_half[c], ACT.Copy).then_inc(uh_ready, 1)

            def gates(c):
                act.wait_ge(unit_used, used(f"ga{c}"))
                if c:
                    act.wait_ge(scan_ready, 1)
                for b in range(4):
                    k = 4 * c + b
                    act.activation(lru_r[:, b, :], ps[:, 4 + b, 0:SEQ], ACT.Sigmoid, bias=col(BA, k))
                    a = act.activation(lru_i[:, b, :], ps[:, 4 + b, SEQ:2 * SEQ], ACT.Sigmoid, bias=col(BX, k))
                a.then_inc(sig_ready, 1)
                act.wait_ge(sig_ready, c + 1)
                for b in range(4):
                    a = act.activation(lru_r[:, b, :], lru_r[:, b, :], ACT.Tanh, scale=lru_c[:, 5, 4 * c + b:4 * c + b + 1])
                a.then_inc(tanh_ready, 1)
                act.wait_ge(tanh_ready, c + 1)
                act.activation(sq_half, lru_r, ACT.Sqrt).then_inc(sqrt_ready, 1)

            split_dense(used("x0") + 2)
            conv_in(0, "x0")
            split_dense(used("x0") + 3)
            conv_out(0)
            split_dense(used("x1") + 2)
            conv_in(1, "x1")
            split_dense(used("ga0") + 2)
            act.wait_ge(lru_ready, 1)
            gates(0)
            conv_out(1)
            split_dense(used("y0") + 2)
            split_dense(used("ga1") + 2)
            gates(1)
            split_dense(used("y1") + 2)
            for c in range(2):
                act.wait_ge(unit_used, used(f"y{c}"))
                act.wait_ge(scan_read, 2)
                act.activation(lru_y[:, 4 * c:4 * c + 4, :], ps[:, 4 * c:4 * c + 4, 0:SEQ],
                               ACT.Gelu_apprx_tanh).then_inc(gelu_ready, 1)
            for c in range(2):
                act.wait_ge(z_ready, c + 1)
                act.activation(xh[:, 4 * c:4 * c + 4, :], lru_h[:, 4 * c:4 * c + 4, :], ACT.Copy).then_inc(zh_ready, 1)
            split_dense(used("ro1") + 2)

            act.wait_ge(rw_in, 16)
            act.activation(rw_h[:], rw[:], ACT.Copy).then_inc(rw_h_ready, 1)
            normalise(4, FFN + 1, 16)
            act.wait_ge(gap_ready, 1)
            act.activation(small[:, 6, :], small[:, 5, :], ACT.Exp).then_inc(gap_exp, 1)

            def gathered_hi(n):
                act.wait_ge(gathered, n + 1)
                for k in range(KD):
                    a = act.activation(xh[:, k, 0:P], ps[:, 6 + k // 4, (k % 4) * P:(k % 4 + 1) * P], ACT.Copy,
                                       scale=col(FFN + 1, k))
                a.then_inc(gh_ready, 1)

            gathered_hi(0)
            act.wait_ge(items_ready, 1)
            extra = act.value_load(ctl[0:1, EXTRA:EXTRA + 1], min_val=0, max_val=EXTRA)
            items = act.snap(extra + E)
            STEPS = FE // CHUNK
            with act.Fori(0, items) as it:
                done = STEPS * it + TB * FSTEPS
                used_base = U_ITEM * it + U0
                at = HI_RING
                split_moe(it, 0, at)
                act.wait_ge(selT_psum, it + 1)
                act.activation(sel_gT, ps[:, 2, 0:SEQ], ACT.Copy).then_inc(selT_ready, 1)
                for j in range(STEPS):
                    u = moe_unit[f"g{j}"][-1] + 1
                    split_moe(it, at, u + 2)
                    at = max(at, u + 2)
                    act.wait_ge(unit_used, used_base + u)
                    act.wait_ge(hT_psum, done + j)
                    act.activation(m_hid, ps[:, j % 2, :], ACT.Silu).then_inc(silu_done, 1)
                    u = moe_unit[f"d{j - 1}" if j else "u0"][-1] + 1
                    split_moe(it, at, u + 2)
                    at = max(at, u + 2)
                    act.wait_ge(hT_psum, done + (j + 1))
                    act.activation(mTh, ps[:, j % 2, :].rearrange("p (k t) -> p k t", t=P), ACT.Copy).then_inc(hTh_ready, 1)
                split_moe(it, at, U_ITEM)
                gathered_hi(it + 1)
                act.wait_ge(unit_used, used_base + U_ITEM)
                act.activation(y_sb[:, 0:BANK], ps[:, 4, :], ACT.Copy).then_inc(y_act, 1)

            act.wait_ge(scattered, items)
            act.dma_start(p_in, p[1, 0].rearrange("(t p) d -> p t d", p=P)).then_inc(p_landed, 16)
            act.dma_start(lnf_row, ln_final.partition_broadcast(P)).then_inc(lnf_in, 16)
            base = U_ITEM * items

            def split_post(first, upto):
                for i in range(first, upto):
                    u = U0 + i
                    g = next(x for x, (name, n) in enumerate(POST) if u in post_unit[name])
                    s = (SHIFT + g) % SLOTS
                    off = (u - post_unit[POST[g][0]][0]) * UNIT
                    act.wait_ge(landed[s], LAND_ITEM * items + (LAND0[s] + 16))
                    act.wait_ge(unit_used, base + (u - HI_RING + 1))
                    act.activation(w_hi[:, u % HI_RING, :], raw[:, s, off:off + UNIT], ACT.Copy).then_inc(hi_done, 1)

            split_post(0, HI_RING)
            act.wait_ge(pT_psum, 2)
            act.activation(pTh, ps[:, 4, :].rearrange("p (k t) -> p k t", k=KP), ACT.Copy).then_inc(pTh_ready, 1)
            act.wait_ge(res_added, 4 * items + 16)
            squares()
            act.wait_ge(mean_ready, 6)
            act.activation(ss[:, 4:6], ss[:, 2:4], ACT.Sqrt).then_inc(root_ready, 1)
            norm_hi(5, PLE + 1)
            split_post(HI_RING, 4)
            embedding_gate(0, base + (U0 + 2), 4 * items + 16)
            split_post(4, 5)
            embedding_gate(1, base + (U0 + 4), 4 * items + 16)
            act.wait_ge(res_added, 4 * items + 20)
            squares()
            act.wait_ge(mean_ready, 7)
            act.activation(ss[:, 4:6], ss[:, 2:4], ACT.Sqrt).then_inc(root_ready, 1)

        @block.vector
        def _(dve):
            chain = [0]

            def link(ins):
                chain[0] += 1
                ins.then_inc(dve_chain, 1)
                dve.wait_ge(dve_chain, chain[0])

            class split:
                at = 0

            def split_dense(upto):
                while split.at < min(upto, U0):
                    u = split.at
                    split.at += 1
                    name, off, n = unit_shape[u]
                    dve.wait_ge(hi_done, u + 1)
                    if u >= LO_RING:
                        dve.wait_ge(unit_used, u - LO_RING + 1)
                    dve.tensor_tensor(w_lo[:, u % LO_RING, 0:n], raw[:, slot_of[name], off:off + n],
                                      w_hi[:, u % HI_RING, 0:n].bitcast(F32), ALU.subtract).then_inc(lo_done, 1)

            def split_moe(it, first, upto):
                for u in range(first, min(upto, U_ITEM)):
                    s = moe_slot[u // 2]
                    off = (u % 2) * UNIT
                    dve.wait_ge(hi_done, U_ITEM * it + (U0 + u + 1))
                    dve.wait_ge(unit_used, U_ITEM * it + (U0 + u - LO_RING + 1))
                    dve.tensor_tensor(w_lo[:, (U0 + u) % LO_RING, :], raw[:, s, off:off + UNIT],
                                      w_hi[:, (U0 + u) % HI_RING, :].bitcast(F32), ALU.subtract).then_inc(lo_done, 1)

            def rest(out, psum, gain, rounded, sem_):
                return dve.scalar_tensor_tensor(out=out, in0=psum, scalar=gain, in1=rounded.bitcast(F32),
                                                op0=ALU.mult, op1=ALU.subtract)

            def norm(n):
                dve.wait_ge(squared, TB * (n + 1))
                dve.tensor_scalar(ss[:, 2:4], ss[:, 0:2], 1.0 / D, EPS, ALU.mult, ALU.add).then_inc(mean_ready, 1)
                dve.wait_ge(root_ready, n + 1)
                link(dve.reciprocal(ss[:, 6:8], ss[:, 4:6]))

            def scale_tokens():
                for t in range(TB):
                    dve.tensor_scalar(xn[:, t, :], res[:, t, :], ss[:, 6 + t:7 + t], None, ALU.mult).then_inc(xn_ready, 1)

            def norm_lo(n, gain):
                for k in range(KD):
                    if k % 2 == 0:
                        dve.wait_ge(xh_ready, 4 * n + k // 2 + 1)
                    a = rest(xl[:, k, :], ps[:, k // 2, (k % 2) * SEQ:(k % 2 + 1) * SEQ], col(gain, k), xh[:, k, :], None)
                    if k % 2:
                        a.then_inc(xl_ready, 1)

            def normalise(n, gain):
                norm(n)
                scale_tokens()
                norm_lo(n, gain)

            def add_residual(b, t, n, before):
                if before is not None:
                    dve.wait_ge(res_added, before)
                dve.tensor_tensor(res[:, t, n * BANK:(n + 1) * BANK], res[:, t, n * BANK:(n + 1) * BANK],
                                  ps[:, b, :], ALU.add).then_inc(res_added, 1)

            used = lambda name: unit_of[name][-1] + 1

            dve.wait_ge(consts, 6)
            norm(0)
            scale_tokens()
            dve.wait_ge(lam_landed, 64)
            link(dve.tensor_tensor(lam_in[:, 0:2, :], lam_in[:, 0:2, :], lam_in[:, 2:4, :], ALU.mult))
            dve.tensor_reduce(lam_t[:, 0:2], lam_in[:, 0:2, :], AX.X, ALU.add).then_inc(lam_summed, 1)
            dve.wait_ge(lam_exp, 1)
            link(dve.tensor_tensor(lam_t[:, 5:6], lam_t[:, 3:4], lam_t[:, 2:3], ALU.subtract))
            dve.tensor_scalar(lam_t[:, 4:5], lam_t[:, 5:6], LAMBDA_INIT, None, ALU.subtract).then_inc(lam_ready, 1)
            dve.wait_ge(prm_psum, 1)
            dve.tensor_copy(prm[:], ps[:, 7, 0:N_ROWS]).then_inc(prm_ready, 1)
            dve.wait_ge(lam_psum, 1)
            link(dve.tensor_copy(nlam[:], ps[:, 6, 0:1]))
            dve.wait_ge(prm_ready, 1)
            link(dve.tensor_scalar(gsub[:], SUB, 1.0 - LAMBDA_INIT, None, ALU.mult))
            lamb = prm[:, LAM * KD:(LAM + 1) * KD]
            dve.scalar_tensor_tensor(out=lru_c[:, 0, :], in0=lamb, scalar=-1.0, in1=lamb, op0=ALU.mult,
                                     op1=ALU.max).then_inc(lru_exp, 1)
            split_dense(LO_RING)
            norm_lo(0, MIX)
            dve.wait_ge(lru_exp, 2)
            z, s, s2, poly = lru_c[:, 1, :], lru_c[:, 2, :], lru_c[:, 3, :], lru_c[:, 4, :]
            link(dve.tensor_scalar(s, z, 2.0, None, ALU.add))
            link(dve.reciprocal(s, s))
            link(dve.tensor_tensor(s, s, z, ALU.mult))
            link(dve.tensor_tensor(s2, s, s, ALU.mult))
            link(dve.tensor_scalar(poly, s2, 1.0 / 17, None, ALU.mult))
            for n in range(15, 1, -2):
                link(dve.scalar_tensor_tensor(out=poly, in0=poly, scalar=1.0 / n, in1=s2, op0=ALU.add, op1=ALU.mult))
            link(dve.scalar_tensor_tensor(out=poly, in0=poly, scalar=1.0, in1=s, op0=ALU.add, op1=ALU.mult))
            link(dve.tensor_scalar(lru_c[:, 5, :], lamb, -4.0, 0.0, ALU.mult, ALU.max))
            dve.scalar_tensor_tensor(out=lru_c[:, 5, :], in0=poly, scalar=8.0, in1=lru_c[:, 5, :],
                                     op0=ALU.mult, op1=ALU.add).then_inc(lru_ready, 1)

            dve.wait_ge(rope_in, 32)

            def rotate(n, name, banks):
                dve.wait_ge(unit_used, used(name))
                if n:
                    dve.wait_ge(rot_psum, n)
                for t in range(TB):
                    if n or t:
                        dve.wait_ge(rot_ready, TB * n + t)
                    halves = ps[:, banks[t], :].rearrange("p (h a f) -> p h a f", a=2, f=HD // 2)
                    out_b = rot_b.rearrange("p (h a f) -> p h a f", a=2, f=HD // 2)
                    cos_t = cosb[:, t, 0, :].unsqueeze(1).broadcast_to([P, 2 * 8, HD // 2])
                    nsin_t = nsin[:, t, :].unsqueeze(1).broadcast_to([P, 8, HD // 2])
                    sin_t = cosb[:, t, 1, :].unsqueeze(1).broadcast_to([P, 8, HD // 2])
                    dve.tensor_tensor(rot_a.rearrange("p (g f) -> p g f", f=HD // 2),
                                      ps[:, banks[t], :].rearrange("p (g f) -> p g f", f=HD // 2), cos_t, ALU.mult)
                    dve.tensor_tensor(out_b[:, :, 0, :], halves[:, :, 1, :], nsin_t, ALU.mult)
                    link(dve.tensor_tensor(out_b[:, :, 1, :], halves[:, :, 0, :], sin_t, ALU.mult))
                    dve.tensor_tensor(rot[:, t, :], rot_a, rot_b, ALU.add).then_inc(rot_ready, 1)

            split_dense(used("k0") + 1)
            rotate(0, "k0", (4, 5))
            split_dense(used("k1") + 1)
            rotate(1, "k1", (6, 7))
            split_dense(used("q0") + 1)
            rotate(2, "q0", (0, 1))
            split_dense(used("q1") + 1)
            rotate(3, "q1", (2, 3))
            split_dense(used("v0") + 1)
            split_dense(used("v1") + 1)

            def mask_and_max(n):
                qb, h0, nh = tiles[n]
                keys = (qb + 1) * P
                dve.wait_ge(scored, n + 1)
                if n:
                    dve.wait_ge(wT_psum, n)
                m3 = mask[:].unsqueeze(1).broadcast_to([P, nh, P])
                for m in range(2):
                    dst = sc_sb[:, m, :].rearrange("p (h k) -> p h k", h=nh)
                    src = ps[:, 2 * (n % 2) + m, :].rearrange("p (h k) -> p h k", h=nh)
                    if qb:
                        dve.tensor_copy(dst[:, :, 0:qb * P], src[:, :, 0:qb * P])
                    a = dve.tensor_tensor(dst[:, :, qb * P:keys], src[:, :, qb * P:keys], m3, ALU.add)
                a.then_inc(masked, 1)
                dve.wait_ge(masked, n + 1)
                for m in range(2):
                    a = dve.tensor_reduce(mx[:, m, 0:nh], sc_sb[:, m, :].rearrange("p (h k) -> p h k", h=nh), AX.X, ALU.max)
                link(a)
                dve.tensor_scalar(mx[:, :, 0:nh], mx[:, :, 0:nh], -(HD ** -0.5), None, ALU.mult).then_inc(max_ready, 1)

            def weigh(n):
                qb, h0, nh = tiles[n]
                keys = (qb + 1) * P
                dve.wait_ge(exp_ready, n + 1)
                link(dve.reciprocal(rden[:, :, 0:nh], den[:, :, 0:nh]))
                link(dve.tensor_scalar(rden[:, 1, 0:nh], rden[:, 1, 0:nh], nlam[:, 0:1], None, ALU.mult))
                for i in range(nh):
                    a = dve.tensor_scalar(sc_sb[:, 1, i * keys:(i + 1) * keys], sc_sb[:, 1, i * keys:(i + 1) * keys],
                                          rden[:, 1, i:i + 1], None, ALU.mult)
                link(a)
                for i in range(nh):
                    a = dve.scalar_tensor_tensor(out=sc_sb[:, 0, i * keys:(i + 1) * keys],
                                                 in0=sc_sb[:, 0, i * keys:(i + 1) * keys], scalar=rden[:, 0, i:i + 1],
                                                 in1=sc_sb[:, 1, i * keys:(i + 1) * keys], op0=ALU.mult, op1=ALU.add)
                a.then_inc(weighed, 1)

            def o_copy(n, qb):
                dve.wait_ge(pv_done, n)
                for b in range(2):
                    a = dve.tensor_copy(xn[:, qb, b * BANK:(b + 1) * BANK], ps[:, 6 + b, :])
                a.then_inc(o_copied, 1)
            for n in range(len(tiles)):
                mask_and_max(n)
                if n == 2:
                    o_copy(2, 0)
                weigh(n)
            o_copy(len(tiles), 1)
            dve.wait_ge(o_squared, TB)
            dve.tensor_scalar(ss_o[:, 0], ss_o[:, 2], 1.0 / P, SUB_EPS, ALU.mult, ALU.add).then_inc(o_mean, 1)
            dve.wait_ge(o_root, 1)
            link(dve.reciprocal(ss_o[:, 2], ss_o[:, 1]))
            dve.wait_ge(o_copied, 2)
            for t in range(TB):
                o3 = xn[:, t, :].rearrange("p (h e) -> p h e", h=H)
                dve.tensor_tensor(o3, o3, ss_o[:, 2, t, :].unsqueeze(2).broadcast_to([P, H, P]), ALU.mult).then_inc(o_ready, 1)
            for k in range(4):
                dve.wait_ge(oh_ready, k + 1)
                rest(xl[:, 2 * k:2 * k + 2, :], ps[:, k, :].rearrange("p (k t) -> p k t", k=2), gsub[:, 0:1],
                     xh[:, 2 * k:2 * k + 2, :], None).then_inc(ol_ready, 1)
            for c in range(2):
                split_dense(used(f"o{c}") + 1)
                dve.wait_ge(unit_used, used(f"o{c}"))
                for t in range(TB):
                    add_residual(4 + 2 * c + t, t, c, None)

            dve.wait_ge(res_added, 4)
            normalise(1, FFN)
            for j in range(FSTEPS):
                w = fwidth[j]
                split_dense(used(f"u{j}") + 1)
                dve.wait_ge(unit_used, used(f"u{j}"))
                for t in range(TB):
                    dve.wait_ge(silu_done, TB * j + t + 1)
                    dve.tensor_tensor(hid[:, t, 0:w], hid[:, t, 0:w], ps[:, 2 * (1 - j % 2) + t, 0:w],
                                      ALU.mult).then_inc(hid_ready, 1)
                if j:
                    split_dense(used(f"d{j - 1}") + 1)
                for t in range(TB):
                    dve.wait_ge(hTh_ready, TB * j + t + 1)
                    dve.tensor_tensor(hTl[:, 0:w // P, t * P:(t + 1) * P],
                                      ps[:, 2 * (j % 2) + t, 0:w].rearrange("p (k t) -> p k t", t=P),
                                      hTh[:, 0:w // P, t * P:(t + 1) * P].bitcast(F32), ALU.subtract).then_inc(hTl_ready, 1)
            split_dense(used(f"d{FSTEPS - 1}") + 1)
            dve.wait_ge(unit_used, used(f"d{FSTEPS - 1}"))
            for t in range(TB):
                for n in range(2):
                    add_residual(4 + 2 * t + n, t, n, None)

            def embedding(layer, n, us_of, base, split_to):
                dve.wait_ge(pTh_ready, layer + 1)
                dve.tensor_tensor(pTl, ps[:, 4, :].rearrange("p (k t) -> p k t", k=KP), pTh.bitcast(F32),
                                  ALU.subtract).then_inc(pTl_ready, 1)
                normalise(n, PLE + layer)
                split_to()
                dve.wait_ge(unit_used, base + (us_of["pp"][-1] + 1))
                for c in range(2):
                    for t in range(TB):
                        dve.wait_ge(gate_ready, TB * (2 * layer + c) + t + 1)
                        a = dve.tensor_tensor(sig[:, t, :], sig[:, t, :], ps[:, 2 * t + c, :], ALU.mult)
                        link(a)
                        r = res[:, t, c * BANK:(c + 1) * BANK]
                        dve.tensor_tensor(r, r, sig[:, t, :], ALU.add).then_inc(res_added, 1)

            dve.wait_ge(res_added, 8)
            embedding(0, 2, unit_of, 0, lambda: split_dense(used("pp") + 1))

            normalise(3, MIX + 1)

            def conv(c):
                for i in range(CONV - 1):
                    if i == 0:
                        dve.wait_ge(tap_ready, 4 * (c + 1))
                        dve.wait_ge(xp_ready, c + 1)
                    for b in range(4):
                        a = dve.scalar_tensor_tensor(out=u_half[c][:, b, :], in0=xp[:, b, i:i + SEQ],
                                                     scalar=col(CW + i, 4 * c + b), in1=u_half[c][:, b, :],
                                                     op0=ALU.mult, op1=ALU.add)
                    if i < CONV - 2:
                        link(a)
                a.then_inc(conv_ready, 1)

            def conv_lo(c):
                dve.wait_ge(uh_ready, c + 1)
                dve.tensor_tensor(ul, u_half[c], uh.bitcast(F32), ALU.subtract).then_inc(ul_ready, 1)

            def scan(c):
                dve.wait_ge(sig_ready, c + 1)
                dve.tensor_tensor(lru_i, lru_i, u_half[c], ALU.mult)
                dve.wait_ge(sqrt_ready, c + 1)
                link(dve.tensor_scalar(lru_r, lru_r, 1.0, None, ALU.add))
                link(dve.reciprocal(lru_r, lru_r))
                link(dve.tensor_tensor(sq_half, sq_half, lru_r, ALU.mult))
                dve.tensor_scalar(lru_r, lru_r, 2.0, -1.0, ALU.mult, ALU.add)
                dve.scalar_tensor_tensor(out=lru_i, in0=sq_half, scalar=2.0, in1=lru_i, op0=ALU.mult,
                                         op1=ALU.mult).then_inc(scan_read, 1)
                dve.wait_ge(scan_read, c + 1)
                for b in range(4):
                    a = dve.tensor_tensor_scan(lru_h[:, 4 * c + b, :], lru_r[:, b, :], lru_i[:, b, :], 0.0, ALU.mult, ALU.add)
                a.then_inc(scan_ready, 1)

            split_dense(used("x0") + 1)
            conv(0)
            conv_lo(0)
            split_dense(used("x1") + 1)
            conv(1)
            split_dense(used("ga0") + 1)
            conv_lo(1)
            scan(0)
            split_dense(used("y0") + 1)
            split_dense(used("ga1") + 1)
            split_dense(used("y1"))
            scan(1)
            split_dense(used("y1") + 1)
            for c in range(2):
                dve.wait_ge(scan_ready, c + 1)
                dve.wait_ge(gelu_ready, c + 1)
                dve.tensor_tensor(lru_h[:, 4 * c:4 * c + 4, :], lru_h[:, 4 * c:4 * c + 4, :],
                                  lru_y[:, 4 * c:4 * c + 4, :], ALU.mult).then_inc(z_ready, 1)
            for c in range(2):
                dve.wait_ge(zh_ready, c + 1)
                dve.tensor_tensor(xl[:, 4 * c:4 * c + 4, :], lru_h[:, 4 * c:4 * c + 4, :],
                                  xh[:, 4 * c:4 * c + 4, :].bitcast(F32), ALU.subtract).then_inc(zl_ready, 1)
            for c in range(2):
                split_dense(used(f"ro{c}") + 1)
                dve.wait_ge(unit_used, used(f"ro{c}"))
                for t in range(TB):
                    add_residual(2 * c + t, t, c, None)

            dve.wait_ge(rw_h_ready, 1)
            dve.tensor_tensor(rw_l[:], rw[:], rw_h[:].bitcast(F32), ALU.subtract).then_inc(rw_l_ready, 1)
            dve.wait_ge(res_added, 16)
            normalise(4, FFN + 1)
            logit, eq, one, second, chose, gate, left, rank = (route[:, i] for i in range(8))
            top1, top2, m = small[:, 0, :], small[:, 1, :], small[:, 2, :]
            wide = lambda a: a.unsqueeze(2).broadcast_to([P, TB, E])

            def first_of_max(values, best, onehot):
                link(dve.tensor_reduce(best, values, AX.X, ALU.max))
                link(dve.tensor_tensor(eq, values, wide(best), ALU.is_equal))
                link(dve.tensor_tensor(eq, eq, rev[:], ALU.mult))
                link(dve.tensor_reduce(m, eq, AX.X, ALU.max))
                link(dve.tensor_tensor(onehot, eq, wide(m), ALU.is_equal))

            dve.wait_ge(logits_ready, 1)
            link(dve.tensor_copy(logit, ps[:, 4:6, 0:E]))
            first_of_max(logit, top1, one)
            link(dve.scalar_tensor_tensor(out=left, in0=one, scalar=NEG, in1=logit, op0=ALU.mult, op1=ALU.add))
            first_of_max(left, top2, second)
            dve.tensor_tensor(chose, one, second, ALU.add).then_inc(chosen, 1)
            dve.tensor_tensor(small[:, 5, :], top2, top1, ALU.subtract).then_inc(gap_ready, 1)
            dve.wait_ge(gap_exp, 1)
            link(dve.tensor_scalar(small[:, 7, :], small[:, 6, :], 1.0, None, ALU.add))
            link(dve.reciprocal(small[:, 7, :], small[:, 7, :]))
            link(dve.tensor_tensor(small[:, 6, :], small[:, 6, :], small[:, 7, :], ALU.mult))
            link(dve.tensor_tensor(gate, one, wide(small[:, 7, :]), ALU.mult))
            link(dve.tensor_tensor(eq, second, wide(small[:, 6, :]), ALU.mult))
            link(dve.tensor_tensor(gate, gate, eq, ALU.add))
            dve.wait_ge(ranked, 1)
            link(dve.tensor_copy(rank, ps[:, 6:8, 0:E]))
            link(dve.scalar_tensor_tensor(out=rank, in0=rank, scalar=1.0, in1=chose, op0=ALU.add, op1=ALU.mult))
            link(dve.tensor_scalar(rank, rank, -1.0, None, ALU.add))
            full, number, pick, lst = over[:, 0, :], over[:, 1, :], over[:, 2, :], over[:, 3, :]
            link(dve.tensor_scalar(full, ps[:, 5, 0:E], float(P), None, ALU.is_gt))
            link(dve.tensor_tensor_scan(number, ones[:, 0:E], full, 0.0, ALU.mult, ALU.add))
            dve.tensor_copy(ctl_f[:, EXTRA:EXTRA + 1], number[:, E - 1:E])
            dve.tensor_copy(item_pos[:, :, 0:E], rank)
            dve.tensor_copy(item_gate[:, :, 0:E], gate)
            dve.memset(item_pos[:, :, ITEMS:], -1.0)
            dve.memset(item_gate[:, :, ITEMS:], 0.0)
            for i in range(EXTRA):
                link(dve.scalar_tensor_tensor(out=pick, in0=number, scalar=float(i + 1), in1=full,
                                              op0=ALU.is_equal, op1=ALU.mult))
                link(dve.scalar_tensor_tensor(out=lst, in0=rev[:, 0, :], scalar=float(E), in1=pick,
                                              op0=ALU.subtract, op1=ALU.mult))
                link(dve.tensor_reduce(ctl_f[:, i:i + 1], lst, AX.X, ALU.add))
                wide_pick = pick.unsqueeze(1).broadcast_to([P, TB, E])
                link(dve.tensor_tensor(eq, rank, wide_pick, ALU.mult))
                link(dve.tensor_reduce(item_pos[:, :, E + i], eq, AX.X, ALU.add))
                link(dve.tensor_tensor(eq, gate, wide_pick, ALU.mult))
                link(dve.tensor_reduce(item_gate[:, :, E + i], eq, AX.X, ALU.add))
            link(dve.tensor_scalar(item_pos[:, :, E:ITEMS], item_pos[:, :, E:ITEMS], -float(P), None, ALU.add))
            link(dve.tensor_scalar(ctl_f[:, 0:EXTRA], ctl_f[:, 0:EXTRA], -1.0, None, ALU.mult))
            dve.tensor_copy(ctl[:], ctl_f[:]).then_inc(items_ready, 1)

            def one_hots(n):
                one = bass.ds(n, 1)
                dve.tensor_copy(cur[:, 0:TB].unsqueeze(2), item_pos[:, :, one])
                dve.tensor_copy(cur[:, TB:2 * TB].unsqueeze(2), item_gate[:, :, one]).then_inc(cur_ready, 1)
                dve.wait_ge(cur_ready, n + 1)
                for t in range(TB):
                    dve.tensor_scalar(sel[:, t, :], iota_row[:], cur[:, t:t + 1], None, ALU.is_equal)
                    a = dve.tensor_scalar(sel_g[:, t, :], iota_row[:], cur[:, t:t + 1], cur[:, TB + t:TB + t + 1],
                                          ALU.is_equal, ALU.mult)
                a.then_inc(sel_ready, 1)

            def gathered_lo(n):
                dve.wait_ge(gh_ready, n + 1)
                for k in range(KD):
                    a = rest(xl[:, k, 0:P], ps[:, 6 + k // 4, (k % 4) * P:(k % 4 + 1) * P], col(FFN + 1, k),
                             xh[:, k, 0:P], None)
                a.then_inc(gl_ready, 1)

            one_hots(0)
            gathered_lo(0)
            dve.wait_ge(items_ready, 1)
            extra = dve.value_load(ctl[0:1, EXTRA:EXTRA + 1], min_val=0, max_val=EXTRA)
            items = dve.snap(extra + E)
            STEPS = FE // CHUNK
            with dve.Fori(0, items) as it:
                done = STEPS * it + TB * FSTEPS
                used_base = U_ITEM * it + U0
                at = 0
                for j in range(STEPS):
                    u = moe_unit[f"u{j}"][-1] + 1
                    split_moe(it, at, u + 1)
                    at = max(at, u + 1)
                    dve.wait_ge(unit_used, used_base + u)
                    dve.wait_ge(silu_done, done + (j + 1))
                    dve.tensor_tensor(m_hid, m_hid, ps[:, 1 - j % 2, :], ALU.mult).then_inc(hid_ready, 1)
                    if j:
                        u = moe_unit[f"d{j - 1}"][-1] + 1
                        split_moe(it, at, u + 1)
                        at = max(at, u + 1)
                    dve.wait_ge(hTh_ready, done + (j + 1))
                    dve.tensor_tensor(mTl, ps[:, j % 2, :].rearrange("p (k t) -> p k t", t=P), mTh.bitcast(F32),
                                      ALU.subtract).then_inc(hTl_ready, 1)
                    if j == 2:
                        dve.wait_ge(selT_psum, it + 1)
                        one_hots(it + 1)
                split_moe(it, at, U_ITEM)
                gathered_lo(it + 1)
                dve.wait_ge(unit_used, used_base + U_ITEM)
                dve.tensor_copy(y_sb[:, BANK:D], ps[:, 5, :]).then_inc(y_dve, 1)
                dve.wait_ge(scattered, it + 1)
                dve.wait_ge(res_added, 4 * it + 16)
                for t in range(TB):
                    for n in range(2):
                        add_residual(scatter_banks[2 * t + n], t, n, None)

            base = U_ITEM * items

            def split_post(first, upto):
                for i in range(first, upto):
                    u = U0 + i
                    g = next(x for x, (name, n) in enumerate(POST) if u in post_unit[name])
                    s = (SHIFT + g) % SLOTS
                    off = (u - post_unit[POST[g][0]][0]) * UNIT
                    dve.wait_ge(hi_done, base + (u + 1))
                    dve.wait_ge(unit_used, base + (u - LO_RING + 1))
                    dve.tensor_tensor(w_lo[:, u % LO_RING, :], raw[:, s, off:off + UNIT],
                                      w_hi[:, u % HI_RING, :].bitcast(F32), ALU.subtract).then_inc(lo_done, 1)

            split_post(0, LO_RING)
            dve.wait_ge(res_added, 4 * items + 16)
            embedding(1, 5, post_unit, base, lambda: split_post(LO_RING, 5))

            norm(6)
            dve.wait_ge(lnf_in, 16)
            for t in range(TB):
                dve.scalar_tensor_tensor(out=xn[:, t, :], in0=res[:, t, :], scalar=ss[:, 6 + t:7 + t], in1=lnf_row,
                                         op0=ALU.mult, op1=ALU.mult).then_inc(final_ready, 1)


def rope_table():
    f32 = np.float32
    inv = f32(1.0) / np.power(f32(10000.0), np.arange(0, HD, 2, dtype=f32) / f32(HD)).astype(f32)
    angle = np.arange(SEQ, dtype=f32)[:, None] * inv[None, :]
    return np.ascontiguousarray(np.stack([np.cos(angle), np.sin(angle), -np.sin(angle)], axis=1).astype(f32))


NAMES = ["x", "p", "ln_mix", "ln_ffn", "ln_ple", "ln_final", "ple_w_proj", "ple_w_gate", "attn_wq", "attn_wk",
         "attn_wv", "attn_wo", "attn_lambda_q1", "attn_lambda_k1", "attn_lambda_q2", "attn_lambda_k2", "attn_subln",
         "ffn_w_gate", "ffn_w_up", "ffn_w_down", "lru_w_in_x", "lru_w_in_y", "lru_conv_w", "lru_conv_b",
         "lru_gate_a_w", "lru_gate_a_b", "lru_gate_x_w", "lru_gate_x_b", "lru_lambda", "lru_w_out", "moe_w_router",
         "moe_w_gate", "moe_w_up", "moe_w_down"]


def kernel(**inputs):
    import concourse.bacc as bacc
    from concourse.bass_utils import run_bass_kernel_spmd

    nc = bacc.Bacc("TRN2", target_bir_lowering=False, num_devices=1)
    arrays, args = {}, {}
    for name in NAMES:
        arrays[f"in_{name}"] = np.ascontiguousarray(inputs[name])
    arrays["in_rope"] = rope_table()
    for name, a in arrays.items():
        args[name[3:]] = nc.dram_tensor(name, a.shape, mybir.dt.from_np(a.dtype), kind="ExternalInput").ap()
    args["out"] = nc.dram_tensor("out_0", (1, SEQ, D), F32, kind="ExternalOutput").ap()
    build(nc, **args)
    r = run_bass_kernel_spmd(nc, [arrays], core_ids=[0])
    return r.results[0]["out_0"]
```

```python
import math
from contextlib import ExitStack

import numpy as np
import concourse.bass as bass
from concourse import mybir

F32 = mybir.dt.float32
F32R = mybir.dt.float32r
I32 = mybir.dt.int32
ALU = mybir.AluOpType
ACT = mybir.ActivationFunctionType
AX = mybir.AxisListType

P = 128
SEQ = 256
TB = SEQ // P
D = 1024
KD = D // P
BANK = 512
H = 8
HD = D // H // 2
FF = 2816
E = 8
FE = 3584
DP = 256
KP = DP // P
CONV = 4
EPS = 1e-6
SUB_EPS = 1e-5
LAMBDA_INIT = 0.8 - 0.6 * math.exp(-0.3 * 0)
NEG = -1e30

SLOTS = 7
SLOT = 4096
UNIT = 2048
HI_RING = 3
LO_RING = 2
CHUNK = 512
EXTRA = 3
ITEMS = E + EXTRA


def plan():
    order = [(n, 2) for n in ("k0", "k1", "q0", "q1", "v0")] + [None, None, ("v1", 2), ("o0", 2), ("o1", 2)]
    steps = -(-FF // CHUNK)
    for j in range(steps):
        n = 2 if (j + 1) * CHUNK <= FF else 1
        order += [(f"g{j}", n), (f"u{j}", n)]
        if j:
            order.append((f"d{j - 1}", 2))
    order.append((f"d{steps - 1}", n))
    order += [("pp", 1), ("pg0", 2), ("pg1", 2), None]
    order += [("x0", 2), ("x1", 2), None, ("ga0", 1), ("y0", 2), ("ga1", 1), ("y1", 2), ("ro0", 2), ("ro1", 2), None]
    return order


def moe_plan():
    steps = FE // CHUNK
    names = []
    for j in range(steps):
        names += [f"g{j}", f"u{j}"] + ([f"d{j - 1}"] if j else [])
    return names + [f"d{steps - 1}"]


def build(nc, x, p, ln_mix, ln_ffn, ln_ple, ln_final, ple_w_proj, ple_w_gate,
          attn_wq, attn_wk, attn_wv, attn_wo, attn_lambda_q1, attn_lambda_k1,
          attn_lambda_q2, attn_lambda_k2, attn_subln, ffn_w_gate, ffn_w_up, ffn_w_down,
          lru_w_in_x, lru_w_in_y, lru_conv_w, lru_conv_b, lru_gate_a_w, lru_gate_a_b,
          lru_gate_x_w, lru_gate_x_b, lru_lambda, lru_w_out,
          moe_w_router, moe_w_gate, moe_w_up, moe_w_down, rope, out):
    slot_of, unit_of = {}, {}
    landed_of, unit_shape = {}, {}
    count = [[0, 0] for s in range(SLOTS)]
    previous = {}
    owner = [None] * SLOTS
    position = n_units = 0
    dense = []
    for entry in plan():
        s = position % SLOTS
        position += 1
        if entry is None:
            continue
        name, n = entry
        slot_of[name], unit_of[name] = s, list(range(n_units, n_units + n))
        n_units += n
        previous[name] = owner[s]
        owner[s] = name
        dense.append(name)
        for i, u in enumerate(unit_of[name]):
            unit_shape[u] = (name, i * UNIT, UNIT // 2 if name.startswith("ga") else UNIT)
            count[s][i] += 2 if name.startswith("ga") else 1
            landed_of[u] = 16 * count[s][i]
    U0 = n_units
    SHIFT = position % SLOTS
    assert SHIFT == 0
    MOE = moe_plan()
    G_ITEM, U_ITEM = len(MOE), 2 * len(MOE)
    assert G_ITEM % SLOTS == 0 and U_ITEM % HI_RING == 0 and U_ITEM % LO_RING == 0
    moe_unit = {n: [2 * i, 2 * i + 1] for i, n in enumerate(MOE)}
    moe_slot = [(SHIFT + i) % SLOTS for i in range(G_ITEM)]
    LAND0 = [[16 * c for c in cs] for cs in count]
    LAND_ITEM = 16 * (G_ITEM // SLOTS)
    moe_unit_abs = {n: [U0 + u for u in us] for n, us in moe_unit.items()}
    post_unit = {"pp": [U0], "pg0": [U0 + 1, U0 + 2], "pg1": [U0 + 3, U0 + 4]}
    scatter_banks = (2, 6, 3, 7)
    tiles = [(0, 0, 4), (0, 4, 4), (1, 0, 2), (1, 2, 2), (1, 4, 2), (1, 6, 2)]

    parts = [(0, 0, 8, 2), (1, 0, 4, 4), (1, 4, 4, 6)]

    def columns(w, n0, n):
        return w[:, n0:n0 + n].rearrange("(k p) n -> p k n", p=P)

    def rows(w, r0, n):
        return w[r0:r0 + n, :].rearrange("(k p) n -> p k n", p=P)

    source = {}
    for c in range(2):
        for n, w in (("k", attn_wk), ("q", attn_wq), ("v", attn_wv), ("o", attn_wo)):
            source[f"{n}{c}"] = columns(w[0], c * CHUNK, CHUNK)
        for n, w in (("x", lru_w_in_x), ("y", lru_w_in_y)):
            source[f"{n}{c}"] = columns(w[0], c * CHUNK, CHUNK)
        source[f"ro{c}"] = rows(lru_w_out[0], c * CHUNK, CHUNK)
        source[f"pg{c}"] = columns(ple_w_gate[0], c * CHUNK, CHUNK)
    source["pp"] = rows(ple_w_proj[0], 0, DP)
    FSTEPS = -(-FF // CHUNK)
    fwidth = [min(CHUNK, FF - j * CHUNK) for j in range(FSTEPS)]
    for j, w in enumerate(fwidth):
        source[f"g{j}"] = columns(ffn_w_gate[0], j * CHUNK, w)
        source[f"u{j}"] = columns(ffn_w_up[0], j * CHUNK, w)
        source[f"d{j}"] = rows(ffn_w_down[0], j * CHUNK, w)

    with ExitStack() as ctx:
        def sb(name, shape, dt=F32):
            return ctx.enter_context(nc.sbuf_tensor(name, shape, dt))

        def sem(name):
            return ctx.enter_context(nc.semaphore(name))

        raw = sb("raw", [P, SLOTS, SLOT])
        w_hi = sb("w_hi", [P, HI_RING, UNIT], F32R)
        w_lo = sb("w_lo", [P, LO_RING, UNIT], F32R)
        res = sb("res", [P, TB, D])
        xn = sb("xn", [P, TB, D])
        xh = sb("xh", [P, KD, SEQ], F32R)
        xl = sb("xl", [P, KD, SEQ], F32R)
        region = sb("region", [P, 2560])
        region_r = sb("region_r", [P, 2048], F32R)
        ident = sb("ident", [P, P])
        tri = sb("tri", [P, P])
        ones = sb("ones", [P, P])
        iota_row = sb("iota_row", [P, P])
        mask = sb("mask", [P, P])
        N_ROWS = 3 * 2 * KD + (CONV + 4) * KD + 1
        rows_in = sb("rows_in", [P, P])
        prm = sb("prm", [P, N_ROWS])
        gsub = sb("gsub", [P, 1])
        lam_t = sb("lam_t", [1, 8])
        nlam = sb("nlam", [P, 1])
        ss = sb("ss", [P, 8])
        ss_o = sb("ss_o", [P, 3, TB, H])
        ss_half = sb("ss_half", [P, 2, TB])
        mx = sb("mx", [P, 2, 2, 4])
        den = sb("den", [P, 2, 2, 4])
        rden = sb("rden", [P, 2, 2, 4])
        lru_c = sb("lru_c", [P, 6, KD])
        rw = sb("rw", [P, KD, E])
        rw_h = sb("rw_h", [P, KD, E], F32R)
        rw_l = sb("rw_l", [P, KD, E], F32R)
        small = sb("small", [P, 16, TB])
        rev = sb("rev", [P, TB, E])
        item_pos = sb("item_pos", [P, TB, ITEMS + 2])
        item_gate = sb("item_gate", [P, TB, ITEMS + 2])
        over = sb("over", [P, 6, E])
        ctl_f = sb("ctl_f", [P, EXTRA + 1])
        ctl = sb("ctl", [P, EXTRA + 1], I32)
        cur = sb("cur", [P, 2 * TB])
        ps = ctx.enter_context(nc.psum_tensor("ps", [P, 8, BANK], F32))

        def col(which, k):
            return prm[:, which * KD + k:which * KD + k + 1]
        MIX, FFN, PLE, CW, CB, BA, BX, LAM = 0, 2, 4, 6, 10, 11, 12, 13
        SUB = prm[:, N_ROWS - 1:N_ROWS]

        scratch = raw[:, SLOTS - 2, :]
        rot_a = scratch[:, 0:1024].rearrange("p (t n) -> p t n", t=TB)
        rot_b = scratch[:, 1024:2048].rearrange("p (t n) -> p t n", t=TB)
        rot = xn[:, 1, :].rearrange("p (t n) -> p t n", t=TB)
        sc_sb = [scratch[:, 2048 + 1024 * i:3072 + 1024 * i].rearrange("p (m n) -> p m n", m=2) for i in range(2)]
        qT = raw[:, SLOTS - 1, 0:KD * SEQ].rearrange("p (k t) -> p k t", k=KD)
        kT = raw[:, SLOTS - 1, KD * SEQ:2 * KD * SEQ].rearrange("p (k t) -> p k t", k=KD)
        v_sb = region[:, 0:TB * D].rearrange("p (t n) -> p t n", t=TB)
        wT = [region[:, TB * D:TB * D + BANK], scratch[:, 0:BANK]]
        lam_in = region[0:1, 0:4 * HD].rearrange("p (i n) -> p i n", i=4)
        rope_sb = xn[:, 0, 0:TB * 3 * (HD // 2)].rearrange("p (t a f) -> p t a f", t=TB, a=3)
        route = region[:, 2304:2432].rearrange("p (i t e) -> p i t e", i=8, t=TB)
        logitT = region[0:E, 0:SEQ]
        hid = region[:, 0:TB * CHUNK].rearrange("p (t n) -> p t n", t=TB)
        hTh = region_r[:, 0:1024].rearrange("p (k t) -> p k t", k=4)
        hTl = region_r[:, 1024:2048].rearrange("p (k t) -> p k t", k=4)
        p_in = [region[:, c:c + TB * DP].rearrange("p (t n) -> p t n", t=TB) for c in (1024, 512)]
        sig = region[:, 0:TB * BANK].rearrange("p (t n) -> p t n", t=TB)
        pTh = [region_r[:, c:c + KP * SEQ].rearrange("p (k t) -> p k t", k=KP) for c in (512, 1024)]
        pTl = [region_r[:, c:c + KP * SEQ].rearrange("p (k t) -> p k t", k=KP) for c in (1536, 1536)]
        XPW = SEQ + CONV - 1
        xp = region[:, 0:4 * XPW].rearrange("p (c t) -> p c t", c=4)
        four = lambda a: a.rearrange("p (c t) -> p c t", c=4)
        u_half = [four(region[:, 1152:2176]), four(raw[:, SLOTS - 1, 2048:3072])]
        sq_half = four(raw[:, SLOTS - 1, 3072:4096])
        uh, ul = four(region_r[:, 0:1024]), four(region_r[:, 1024:2048])
        lru_h = raw[:, SLOTS - 1, 0:2048].rearrange("p (k t) -> p k t", k=KD)
        lru_r = [four(xn[:, 0, :]), four(region[:, 0:1024])]
        lru_i = [four(xn[:, 1, :]), lru_h[:, 4:8, :]]
        lru_iu = [lru_i[0], u_half[1]]
        lru_y = [u_half[0], four(xn[:, 1, :])]
        sel = region[:, 0:256].rearrange("p (t s) -> p t s", t=TB)
        sel_g = region[:, 256:512].rearrange("p (t s) -> p t s", t=TB)
        sel_gT = region[:, 512:768]
        m_hid = region[:, 768:1280]
        y_sb = region[:, 1280:2304]
        mTh = region_r[:, 0:512].rearrange("p (k t) -> p k t", k=4)
        mTl = region_r[:, 512:1024].rearrange("p (k t) -> p k t", k=4)
        lnf_row = region[:, 1536:2560]

        landed = [[sem(f"landed{s}_{h}") for h in range(2)] for s in range(SLOTS)]
        hi_done, lo_done, unit_used = sem("hi_done"), sem("lo_done"), sem("unit_used")
        x_in, x_in1, mix_landed, rows_landed, rope_in, lam_landed, rw_in, p_landed, lnf_in, stored = map(sem, (
            "x_in", "x_in1", "mix_landed", "rows_landed", "rope_in", "lam_landed", "rw_in", "p_landed", "lnf_in", "stored"))
        zeroed, consts = sem("zeroed"), sem("consts")
        prm_psum, prm_ready = sem("prm_psum"), sem("prm_ready")
        lam_summed, lam_exp, lam_ready, lam_psum, nlam_ready = map(sem, (
            "lam_summed", "lam_exp", "lam_ready", "lam_psum", "nlam_ready"))
        lru_exp, lru_ready = sem("lru_exp"), sem("lru_ready")
        dve_chain = sem("dve_chain")
        squared, mean_ready, root_ready, rstd_ready, xn_ready = map(sem, (
            "squared", "mean_ready", "root_ready", "rstd_ready", "xn_ready"))
        xT_psum, xh_ready, xl_ready = map(sem, ("xT_psum", "xh_ready", "xl_ready"))
        rot_parts, rot_ready, rot_psum, qk_ready, v_ready = map(sem, (
            "rot_parts", "rot_ready", "rot_psum", "qk_ready", "v_ready"))
        scored, masked, max_ready, exp_ready, weighed, wT_psum, wT_ready, pv_done = map(sem, (
            "scored", "masked", "max_ready", "exp_ready", "weighed", "wT_psum", "wT_ready", "pv_done"))
        o_squared, o_copied, o_mean, o_root, o_ready, oT_psum, oh_ready, ol_ready, res_added = map(sem, (
            "o_squared", "o_copied", "o_mean", "o_root", "o_ready", "oT_psum", "oh_ready", "ol_ready", "res_added"))
        silu_done, hid_ready, hT_psum, hTh_ready, hTl_ready = map(sem, (
            "silu_done", "hid_ready", "hT_psum", "hTh_ready", "hTl_ready"))
        pT_psum, pTh_ready, pTl_ready, gate_ready = map(sem, (
            "pT_psum", "pTh_ready", "pTl_ready", "gate_ready"))
        xp_zero, xp_ready, conv_ready, scan_in, uh_ready, ul_ready = map(sem, (
            "xp_zero", "xp_ready", "conv_ready", "scan_in", "uh_ready", "ul_ready"))
        in_gate_ready = sem("in_gate_ready")
        sig_ready, tanh_ready, sqrt_ready, scan_read, scan_ready, gelu_ready, z_ready, zh_ready, zl_ready = map(sem, (
            "sig_ready", "tanh_ready", "sqrt_ready", "scan_read", "scan_ready", "gelu_ready", "z_ready", "zh_ready", "zl_ready"))
        rw_h_ready, rw_l_ready, logitT_psum, logitT_ready, logits_ready, gap_ready, gap_exp, chosen, ranked, items_ready = map(sem, (
            "rw_h_ready", "rw_l_ready", "logitT_psum", "logitT_ready", "logits_ready", "gap_ready", "gap_exp", "chosen", "ranked", "items_ready"))
        cur_ready, sel_ready, selT_psum, selT_ready, gathered, gh_ready, gl_ready, y_act, y_dve, scattered = map(sem, (
            "cur_ready", "sel_ready", "selT_psum", "selT_ready", "gathered", "gh_ready", "gl_ready",
            "y_act", "y_dve", "scattered"))
        final_ready = sem("final_ready")

        block = ctx.enter_context(nc.Block())

        @block.sync
        def _(sp):
            def load_unit(s, half, src):
                n = src.shape[1] * src.shape[2]
                dst = raw[:, s, half * UNIT:half * UNIT + n].rearrange("p (k n) -> p k n", k=src.shape[1])
                sp.dma_start(dst, src).then_inc(landed[s][half], 16)

            def load_dense(name):
                if previous[name]:
                    sp.wait_ge(lo_done, unit_of[previous[name]][-1] + 1)
                if name == "g1":
                    sp.wait_ge(pv_done, len(tiles))
                s = slot_of[name]
                if name.startswith("ga"):
                    c = int(name[2])
                    for i, w in enumerate((lru_gate_a_w, lru_gate_x_w)):
                        dst = raw[:, s, i * BANK:(i + 1) * BANK].rearrange("p (n d) -> p n d", n=4)
                        sp.dma_start(dst, w[0, 4 * c:4 * c + 4].rearrange("n c d -> c n d")).then_inc(landed[s][0], 16)
                    return
                src = source[name]
                k = src.shape[1] // len(unit_of[name])
                for i in range(len(unit_of[name])):
                    load_unit(s, i, src[:, i * k:(i + 1) * k, :])

            def load_item(it, e):
                for i, name in enumerate(MOE):
                    s = moe_slot[i]
                    j = int(name[1:])
                    one = bass.ds(e, 1)
                    for half in range(2):
                        if i >= SLOTS:
                            sp.wait_ge(lo_done, U_ITEM * it + (U0 + 2 * (i - SLOTS) + half + 1))
                        elif not isinstance(it, int):
                            sp.wait_ge(lo_done, U_ITEM * it + (U0 - U_ITEM + 2 * (i + G_ITEM - SLOTS) + half + 1))
                        elif owner[s]:
                            sp.wait_ge(lo_done, unit_of[owner[s]][-1] + 1)
                            if s == SLOTS - 1:
                                sp.wait_ge(zl_ready, 4)
                        if name[0] == "d":
                            r = j * CHUNK + half * 2 * P
                            src = moe_w_down[0][one, r:r + 2 * P, :].rearrange("e (k p) n -> p (e k) n", p=P)
                        else:
                            w = moe_w_gate if name[0] == "g" else moe_w_up
                            src = w[0][one, half * D // 2:(half + 1) * D // 2,
                                       j * CHUNK:(j + 1) * CHUNK].rearrange("e (k p) n -> p (e k) n", p=P)
                        load_unit(s, half, src)

            for t in range(TB):
                sp.dma_start(res[:, t, :], x[0, t * P:(t + 1) * P, :]).then_inc((x_in, x_in1)[t], 16)
            load_dense(dense[0])
            at = 2 * KD
            for w, n in ((ln_ffn, 2 * KD), (ln_ple, 2 * KD)):
                sp.dma_start(rows_in[at:at + n, :], w.rearrange("l (k p) -> (l k) p", p=P)).then_inc(rows_landed, 16)
                at += n
            sp.dma_start(rows_in[at:at + CONV * KD, :],
                         lru_conv_w[0].rearrange("i (k p) -> (i k) p", p=P)).then_inc(rows_landed, 16)
            at += CONV * KD
            for w in (lru_conv_b, lru_gate_a_b, lru_gate_x_b, lru_lambda):
                sp.dma_start(rows_in[at:at + KD, :], w.rearrange("l (k p) -> (l k) p", p=P)).then_inc(rows_landed, 16)
                at += KD
            sp.dma_start(rows_in[at:at + 1, :], attn_subln).then_inc(rows_landed, 16)
            sp.dma_start(rope_sb, rope.rearrange("(t p) a f -> p t a f", p=P)).then_inc(rope_in, 16)
            for name in dense[1:]:
                load_dense(name)
            load_item(0, 0)
            with sp.Fori(1, E) as it:
                load_item(it, it)
            sp.wait_ge(items_ready, 1)
            extra = sp.value_load(ctl[0:1, EXTRA:EXTRA + 1], min_val=0, max_val=EXTRA)
            with sp.If(extra > 0):
                with sp.Fori(0, extra) as i:
                    e = sp.value_load(ctl[0:1, bass.ds(i, 1)], min_val=0, max_val=E - 1)
                    load_item(i + E, e)
            items = sp.snap(extra + E)
            post_source = [rows(ple_w_proj[1], 0, DP)]
            for c in range(2):
                w = columns(ple_w_gate[1], c * CHUNK, CHUNK)
                post_source += [w[:, 0:KD // 2, :], w[:, KD // 2:KD, :]]
            for u, src in enumerate(post_source):
                sp.wait_ge(lo_done, U_ITEM * items + (U0 - U_ITEM + 2 * (G_ITEM - SLOTS) + u + 1))
                load_unit(u // 2, u % 2, src)
            for i in range(2 * TB):
                t, h = i // 2, slice(i % 2 * BANK, (i % 2 + 1) * BANK)
                sp.wait_ge(final_ready, i + 1)
                sp.dma_start(out[0].rearrange("(t p) d -> p t d", p=P)[:, t, h], xn[:, t, h]).then_inc(stored, 16)
            sp.wait_ge(stored, 16 * 2 * TB)

        @block.gpsimd
        def _(pool):
            pool.memset(ident[:], 0.0).then_inc(zeroed, 1)
            pool.memset(mask[:], 0.0).then_inc(zeroed, 1)
            pool.memset(tri[:], 1.0).then_inc(zeroed, 1)
            pool.memset(ones[:], 1.0).then_inc(consts, 1)
            pool.wait_ge(zeroed, 3)
            pool.affine_select(out=ident[:], in_=ident[:], compare_op=ALU.not_equal, fill=1.0, base=0,
                               pattern=[[-1, P]], channel_multiplier=1).then_inc(consts, 1)
            pool.affine_select(out=mask[:], in_=mask[:], compare_op=ALU.is_ge, fill=NEG, base=0,
                               pattern=[[-1, P]], channel_multiplier=1).then_inc(consts, 1)
            pool.affine_select(out=tri[:], in_=tri[:], compare_op=ALU.is_ge, fill=0.0, base=-1,
                               pattern=[[1, P]], channel_multiplier=-1).then_inc(consts, 1)
            pool.iota(iota_row[:], [[1, P]], base=0, channel_multiplier=0,
                      allow_small_or_imprecise_dtypes=True).then_inc(consts, 1)
            pool.iota(rev[:], [[0, TB], [-1, E]], base=E, channel_multiplier=0,
                      allow_small_or_imprecise_dtypes=True).then_inc(consts, 1)
            for i, w in enumerate((attn_lambda_q1, attn_lambda_q2, attn_lambda_k1, attn_lambda_k2)):
                pool.dma_start(lam_in[:, i, :], w).then_inc(lam_landed, 16)
            pool.dma_start(rw[:], moe_w_router[0].rearrange("(k p) e -> p k e", p=P)).then_inc(rw_in, 16)
            for n in range(4):
                if n:
                    pool.wait_ge(rot_psum, n)
                for t in range(TB):
                    pool.wait_ge(rot_parts, TB * n + t + 1)
                    pool.tensor_tensor(rot[:, t, :], rot_a[:, t, :], rot_b[:, t, :], ALU.add).then_inc(rot_ready, 1)
            pool.wait_ge(res_added, 12)
            pool.memset(xp[:, :, 0:CONV - 1], 0.0).then_inc(xp_zero, 1)
            for c in range(2):
                pool.wait_ge(in_gate_ready, c + 1)
                pool.wait_ge(conv_ready, c + 1)
                pool.tensor_tensor(lru_iu[c], lru_i[c], u_half[c], ALU.mult).then_inc(scan_read, 1)
            pool.wait_ge(pT_psum, 2)
            pool.wait_ge(zl_ready, 4)
            pool.memset(sel_gT, 0.0).then_inc(selT_ready, 1)
            pool.memset(y_sb[:, 0:BANK], 0.0).then_inc(y_act, 1)
            pool.memset(y_sb[:, BANK:D], 0.0).then_inc(y_dve, 1)

        @block.tensor
        def _(pe):
            def bank(b, c0=0, n=BANK):
                return ps[:, b, c0:c0 + n]

            def hi(u, off, n):
                return w_hi[:, (u % HI_RING), off:off + n]

            def lo(u, off, n):
                return w_lo[:, (u % LO_RING), off:off + n]

            def project(us, base, kind, width, a_hi, a_lo, tbs, banks, k_total, first=True, last=True, fresh=None,
                        halfway=None):
                per = k_total // len(us)
                for i, u in enumerate(us):
                    pieces = []
                    for kk in range(per):
                        k = i * per + kk
                        if kind == "columns":
                            pieces.append((k, 0, kk * width, width))
                        else:
                            pieces += [(k, n, kk * D + n * BANK, BANK) for n in range(2)]
                    pe.wait_ge(hi_done, base + (u + 1))
                    for t in range(tbs):
                        for k, n, off, w in pieces:
                            if fresh is not None and t == 0 and k % 2 == 0:
                                pe.wait_ge(fresh[0], fresh[2] + k // 2 + 1)
                                pe.wait_ge(fresh[1], fresh[2] + k // 2 + 1)
                            b = bank(banks[t][n], 0, w)
                            pe.matmul(b, a_hi[:, k, t * P:(t + 1) * P], hi(u, off, w), start=(first and k == 0), stop=False,
                                      skip_group_check=True)
                            pe.matmul(b, a_lo[:, k, t * P:(t + 1) * P], hi(u, off, w), start=False, stop=False,
                                      skip_group_check=True)
                    pe.wait_ge(lo_done, base + (u + 1))
                    for t in range(tbs):
                        for k, n, off, w in pieces:
                            mm = pe.matmul(bank(banks[t][n], 0, w), a_hi[:, k, t * P:(t + 1) * P], lo(u, off, w),
                                           start=False, stop=(last and k == k_total - 1), skip_group_check=True)
                    mm.then_inc(unit_used, 1)
                    if halfway and i == 0:
                        halfway()

            def turn(src, ready, b0, done, halves=(0, 1)):
                for half in halves:
                    ready(half)
                    for k in range(4 * half, 4 * half + 4):
                        for t in range(TB):
                            tr = pe.transpose(bank(b0 + k // 2, (k % 2) * SEQ + t * P, P), src[:, t, k * P:(k + 1) * P], ident[:])
                        if k % 2:
                            tr.then_inc(done, 1)

            def added(count):
                return lambda half: pe.wait_ge(res_added, count + TB * (half + 1))

            def normed(n):
                return xh_ready, xl_ready, 4 * n

            def gated_ffn(steps, us_of, base, a_hi, a_lo, th, tl, hid_at, tbs, pairs, acc, done, width, fresh=None,
                          between={}):
                for j in range(steps):
                    w = width[j]
                    g_banks = [[pairs[j % 2][t]] for t in range(tbs)]
                    u_banks = [[pairs[1 - j % 2][t]] for t in range(tbs)]
                    if j or not isinstance(done, int) or done:
                        pe.wait_ge(hid_ready, tbs * j + done)
                    project(us_of[f"g{j}"], base, "columns", w, a_hi, a_lo, tbs, g_banks, KD,
                            fresh=None if j else fresh)
                    if j or not isinstance(done, int) or done:
                        pe.wait_ge(hTh_ready, tbs * j + done)
                        pe.wait_ge(hTl_ready, tbs * j + done)
                    project(us_of[f"u{j}"], base, "columns", w, a_hi, a_lo, tbs, u_banks, KD)
                    if j:
                        down(j - 1, us_of, base, th, tl, tbs, acc, steps, width)
                    if j in between:
                        between[j]()
                    for t in range(tbs):
                        pe.wait_ge(hid_ready, tbs * j + (t + 1) + done)
                        for c in range(w // P):
                            tr = pe.transpose(bank(g_banks[t][0], c * P, P), hid_at(t)[:, c * P:(c + 1) * P], ident[:])
                        tr.then_inc(hT_psum, 1)

            def down(j, us_of, base, th, tl, tbs, acc, steps, width):
                project(us_of[f"d{j}"], base, "rows", D, th, tl, tbs, acc, width[j] // P,
                        first=(j == 0), last=(j == steps - 1))

            def transposed_project(name, outs, fresh=None):
                for i, u in enumerate(unit_of[name]):
                    pe.wait_ge(hi_done, u + 1)
                    for c in range(4):
                        for kk in range(4):
                            k = 4 * i + kk
                            if fresh is not None and c == 0 and k % 2 == 0:
                                pe.wait_ge(fresh[0], fresh[2] + k // 2 + 1)
                                pe.wait_ge(fresh[1], fresh[2] + k // 2 + 1)
                            w = hi(u, kk * CHUNK + c * P, P)
                            pe.matmul(outs[c], w, xh[:, k, :], start=(k == 0), stop=False,
                                      skip_group_check=True)
                            pe.matmul(outs[c], w, xl[:, k, :], start=False, stop=False,
                                      skip_group_check=True)
                    pe.wait_ge(lo_done, u + 1)
                    for c in range(4):
                        for kk in range(4):
                            k = 4 * i + kk
                            mm = pe.matmul(outs[c], lo(u, kk * CHUNK + c * P, P), xh[:, k, :],
                                           start=False, stop=(k == KD - 1), skip_group_check=True)
                    mm.then_inc(unit_used, 1)

            def turn_embedding(layer, b):
                pe.wait_ge(p_landed, 16 * (layer + 1))
                for k in range(KP):
                    for t in range(TB):
                        tr = pe.transpose(bank(b, k * SEQ + t * P, P), p_in[layer][:, t, k * P:(k + 1) * P], ident[:])
                tr.then_inc(pT_psum, 1)

            def embedding(layer, us_of, base, norm, ready):
                pe.wait_ge(pTh_ready, layer + 1)
                pe.wait_ge(pTl_ready, layer + 1)
                project(us_of["pp"], base, "rows", D, pTh[layer], pTl[layer], TB, [[0, 1], [2, 3]], KP)
                turn(res, ready, 4, xT_psum)
                for c in range(2):
                    project(us_of[f"pg{c}"], base, "columns", BANK, xh, xl, TB, [[4 + 2 * c], [5 + 2 * c]], KD,
                            fresh=None if c else normed(norm))

            pe.wait_ge(consts, 6)
            pe.wait_ge(mix_landed, 16)
            pe.transpose(bank(7, 0, 2 * KD), rows_in[0:2 * KD, :], ident[0:2 * KD, 0:2 * KD]).then_inc(prm_psum, 1)
            pe.wait_ge(x_in, 16)
            pe.wait_ge(x_in1, 16)
            turn(res, lambda half: None, 0, xT_psum)

            def turn_rows():
                pe.wait_ge(prm_ready, 1)
                pe.wait_ge(rows_landed, 16 * 8)
                pe.transpose(bank(7, 0, N_ROWS), rows_in[0:N_ROWS, :], ident[0:N_ROWS, 0:N_ROWS]).then_inc(prm_psum, 1)

            def rot_transposes(n, banks):
                pe.wait_ge(rot_ready, TB * (n + 1))
                for t in range(TB):
                    for c in range(4):
                        tr = pe.transpose(bank(banks[c // 2], (c % 2) * SEQ + t * P, P), rot[:, t, c * P:(c + 1) * P], ident[:])
                tr.then_inc(rot_psum, 1)

            def attn_project(us, banks, fresh=None, halfway=None):
                project(us, 0, "columns", BANK, xh, xl, TB, [[banks[0]], [banks[1]]], KD, fresh=fresh, halfway=halfway)

            attn_project(unit_of["k0"], (4, 5), fresh=normed(0), halfway=turn_rows)
            pe.wait_ge(prm_ready, 2)
            attn_project(unit_of["k1"], (6, 7))
            rot_transposes(0, (4, 5))
            attn_project(unit_of["q0"], (0, 1))
            rot_transposes(1, (6, 7))
            attn_project(unit_of["q1"], (2, 3))
            rot_transposes(2, (0, 1))
            pe.wait_ge(qk_ready, 1)
            attn_project(unit_of["v0"], (4, 5))
            rot_transposes(3, (2, 3))

            def scores(n):
                qb, h0, nh = tiles[n]
                keys = (qb + 1) * P
                if n < 2:
                    pe.wait_ge(qk_ready, 3 + n)
                if n >= 2:
                    pe.wait_ge(masked, n - 1)
                for m in range(2):
                    for i in range(nh):
                        mm = pe.matmul(bank(2 * (n % 2) + m, i * keys, keys),
                                       qT[m * HD:(m + 1) * HD, h0 + i, qb * P:(qb + 1) * P],
                                       kT[m * HD:(m + 1) * HD, h0 + i, 0:keys], start=True, stop=True)
                mm.then_inc(scored, 1)

            def weights_times_values(n):
                qb, h0, nh = tiles[n]
                pe.wait_ge(weighed, n + 1)
                if n == 0:
                    pe.wait_ge(v_ready, 2)
                for i in range(nh):
                    for kb in range(qb + 1):
                        c = i * (qb + 1) + kb
                        tr = pe.transpose(bank(4 + n % 2, c * P, P), sc_sb[n % 2][:, 0, c * P:(c + 1) * P], ident[:])
                tr.then_inc(wT_psum, 1)
                pe.wait_ge(wT_ready, n + 1)
                if n == 2:
                    pe.wait_ge(o_copied, 1)
                for i in range(nh):
                    h = h0 + i
                    for kb in range(qb + 1):
                        c = i * (qb + 1) + kb
                        mm = pe.matmul(bank(6 + h // 4, (h % 4) * P, P), wT[n % 2][:, c * P:(c + 1) * P],
                                       v_sb[:, kb, h * P:(h + 1) * P], start=(kb == 0), stop=(kb == qb))
                mm.then_inc(pv_done, 1)

            scores(0)
            scores(1)
            pe.wait_ge(qk_ready, 2)
            pe.wait_ge(lam_ready, 1)
            pe.matmul(bank(6, 0, 1), ones[0:1, :], lam_t[0:1, 4:5], start=True, stop=True).then_inc(lam_psum, 1)
            pe.wait_ge(nlam_ready, 1)
            attn_project(unit_of["v1"], (6, 7))
            for n in range(len(tiles)):
                if n == 5:
                    pe.wait_ge(masked, n)
                    turn(xn, lambda half: pe.wait_ge(o_ready, 2), 0, oT_psum, (0,))
                weights_times_values(n)
                if n + 2 < len(tiles):
                    scores(n + 2)
            pe.wait_ge(masked, len(tiles))
            attn_project(unit_of["o0"], (4, 5), fresh=(oh_ready, ol_ready, 0),
                         halfway=lambda: turn(xn, lambda half: pe.wait_ge(o_ready, 3), 0, oT_psum, (1,)))
            attn_project(unit_of["o1"], (6, 7), halfway=lambda: turn(res, added(0), 0, xT_psum, (0,)))

            turn(res, added(0), 0, xT_psum, (1,))
            dense_acc = [[4, 6], [5, 7]]
            gated_ffn(FSTEPS, unit_of, 0, xh, xl, hTh, hTl, lambda t: hid[:, t, :], TB,
                      ((0, 1), (2, 3)), dense_acc, 0, fwidth, fresh=normed(1))
            turn_embedding(0, 0)
            pe.wait_ge(hTh_ready, TB * FSTEPS)
            pe.wait_ge(hTl_ready, TB * FSTEPS)
            down(FSTEPS - 1, unit_of, 0, hTh, hTl, TB, dense_acc, FSTEPS, fwidth)

            embedding(0, unit_of, 0, 2, added(4))

            turn(xn, lambda half: pe.wait_ge(xn_ready, TB * (half + 1)), 4, xT_psum)
            transposed_project("x0", [bank(c, 0, SEQ) for c in range(4)], fresh=normed(3))
            transposed_project("x1", [bank(4 + c, 0, SEQ) for c in range(4)])

            def lru_gates(c):
                u = unit_of[f"ga{c}"][0]
                pe.wait_ge(uh_ready, c + 1)
                pe.wait_ge(hi_done, u + 1)
                pe.wait_ge(ul_ready, c + 1)
                pe.wait_ge(lo_done, u + 1)
                if c:
                    pe.wait_ge(sig_ready, 1)
                for b in range(4):
                    for g in range(2):
                        o = bank(b, g * SEQ, SEQ)
                        w = g * BANK + b * P
                        pe.matmul(o, hi(u, w, P), uh[:, b, :], start=True, stop=False)
                        pe.matmul(o, hi(u, w, P), ul[:, b, :], start=False, stop=False)
                        mm = pe.matmul(o, lo(u, w, P), uh[:, b, :], start=False, stop=True)
                mm.then_inc(unit_used, 1)

            lru_gates(0)
            pe.wait_ge(xp_ready, 2)
            transposed_project("y0", [bank(4 + c, 0, SEQ) for c in range(4)])
            lru_gates(1)
            pe.wait_ge(gelu_ready, 1)
            transposed_project("y1", [bank(4 + c, 0, SEQ) for c in range(4)])
            pe.wait_ge(sig_ready, 2)
            for c in range(2):
                project(unit_of[f"ro{c}"], 0, "rows", D, xh[:, 4 * c:4 * c + 4, :], xl[:, 4 * c:4 * c + 4, :], TB,
                        [[0, 2], [1, 3]], 4, first=(c == 0), last=(c == 1), fresh=(zh_ready, zl_ready, 2 * c))

            turn(res, added(12), 4, xT_psum)
            pe.wait_ge(rw_h_ready, 1)
            pe.wait_ge(rw_l_ready, 1)
            for k in range(KD):
                for i, (a, w) in enumerate(((xh, rw_h), (xl, rw_h), (xh, rw_l))):
                    if k % 2 == 0 and i == 0:
                        pe.wait_ge(xh_ready, 4 * 4 + k // 2 + 1)
                        pe.wait_ge(xl_ready, 4 * 4 + k // 2 + 1)
                    mm = pe.matmul(ps[0:E, 0, 0:SEQ], w[:, k, :], a[:, k, :],
                                   start=(k == 0 and i == 0), stop=(k == KD - 1 and i == 2))
            mm.then_inc(logitT_psum, 1)
            turn_embedding(1, 1)
            pe.wait_ge(logitT_ready, 1)
            for t in range(TB):
                tr = pe.transpose(bank(5, t * E, E), logitT[:, t * P:(t + 1) * P], ident[0:E, 0:E])
            tr.then_inc(logits_ready, 1)
            chose = route[:, 4]
            pe.wait_ge(chosen, 1)
            pe.matmul(bank(6, 0, E), tri[:], chose[:, 0, :], start=True, stop=True)
            pe.matmul(bank(7, 0, E), ones[:], chose[:, 0, :], start=True, stop=False)
            pe.matmul(bank(7, 0, E), tri[:], chose[:, 1, :], start=False, stop=True)
            pe.matmul(bank(5, 0, E), ones[:], chose[:, 0, :], start=True, stop=False)
            pe.matmul(bank(5, 0, E), ones[:], chose[:, 1, :], start=False, stop=True).then_inc(ranked, 1)

            def gather(n):
                pe.wait_ge(sel_ready, n + 1)
                for k in range(KD):
                    for t in range(TB):
                        mm = pe.matmul(bank(6 + k // 4, (k % 4) * P, P), xn[:, t, k * P:(k + 1) * P], sel[:, t, :],
                                       start=(t == 0), stop=(t == TB - 1))
                mm.then_inc(gathered, 1)

            gather(0)
            pe.wait_ge(items_ready, 1)
            extra = pe.value_load(ctl[0:1, EXTRA:EXTRA + 1], min_val=0, max_val=EXTRA)
            items = pe.snap(extra + E)
            STEPS = FE // CHUNK
            moe_acc = [[4, 5]]
            dense_hid = TB * FSTEPS

            def scatter(n):
                pe.wait_ge(y_act, n + 1)
                pe.wait_ge(y_dve, n + 1)
                pe.wait_ge(selT_ready, n + 1)
                pe.wait_ge(res_added, 4 * n + 16)
                for t in range(TB):
                    for c in range(2):
                        mm = pe.matmul(bank(scatter_banks[2 * t + c]), sel_gT[:, t * P:(t + 1) * P],
                                       y_sb[:, c * BANK:(c + 1) * BANK], start=True, stop=True)
                mm.then_inc(scattered, 1)

            def turn_sel(n):
                pe.wait_ge(res_added, 4 * n + 20)
                for t in range(TB):
                    tr = pe.transpose(bank(2, t * P, P), sel_g[:, t, :], ident[:])
                tr.then_inc(selT_psum, 1)

            with pe.Fori(0, items) as it:
                pe.wait_ge(gh_ready, it + 1)
                pe.wait_ge(gl_ready, it + 1)
                gated_ffn(STEPS, moe_unit_abs, U_ITEM * it, xh, xl, mTh, mTl, lambda t: m_hid, 1,
                          ((0,), (1,)), moe_acc, STEPS * it + dense_hid, [CHUNK] * STEPS,
                          between={0: lambda: scatter(it), 1: lambda: turn_sel(it)})
                gather(it + 1)
                pe.wait_ge(hTh_ready, STEPS * it + (dense_hid + STEPS))
                pe.wait_ge(hTl_ready, STEPS * it + (dense_hid + STEPS))
                down(STEPS - 1, moe_unit_abs, U_ITEM * it, mTh, mTl, 1, moe_acc, STEPS, [CHUNK] * STEPS)
            pe.wait_ge(gh_ready, items + 1)
            pe.wait_ge(gl_ready, items + 1)
            scatter(items)

            n_added = 4 * items + 16
            pe.wait_ge(res_added, n_added + 2)
            embedding(1, post_unit, U_ITEM * items, 5, added(n_added))

        @block.scalar
        def _(act):
            class split:
                at = 0

            def split_dense(upto):
                while split.at < min(upto, U0):
                    u = split.at
                    split.at += 1
                    name, off, n = unit_shape[u]
                    s = slot_of[name]
                    act.wait_ge(landed[s][off // UNIT], landed_of[u])
                    if u >= HI_RING:
                        act.wait_ge(unit_used, u - HI_RING + 1)
                    act.activation(w_hi[:, u % HI_RING, 0:n], raw[:, s, off:off + n], ACT.Copy).then_inc(hi_done, 1)

            def split_moe(it, first, upto):
                for u in range(first, min(upto, U_ITEM)):
                    g = u // 2
                    s = moe_slot[g]
                    turn = sum(x == s for x in moe_slot[:g + 1])
                    act.wait_ge(landed[s][u % 2], LAND_ITEM * it + (LAND0[s][u % 2] + 16 * turn))
                    act.wait_ge(unit_used, U_ITEM * it + (U0 + u - HI_RING + 1))
                    off = (u % 2) * UNIT
                    act.activation(w_hi[:, (U0 + u) % HI_RING, :], raw[:, s, off:off + UNIT], ACT.Copy).then_inc(hi_done, 1)

            def squares(junk=lambda t: xn[:, t, :]):
                for t in range(TB):
                    act.activation(junk(t), res[:, t, :], ACT.Square, accum_out=ss[:, t:t + 1]).then_inc(squared, 1)

            def half_squares(c, count):
                for t in range(TB):
                    act.wait_ge(res_added, count + (TB * c + t + 1))
                    h = slice(c * BANK, (c + 1) * BANK)
                    act.activation(xn[:, t, h], res[:, t, h], ACT.Square,
                                   accum_out=ss_half[:, c, t:t + 1]).then_inc(squared, 1)

            def root(n):
                act.wait_ge(mean_ready, n + 1)
                act.activation(ss[:, 4:6], ss[:, 2:4], ACT.Sqrt).then_inc(root_ready, 1)

            def norm_hi(n, gain, b0):
                for k in range(KD):
                    if k % 2 == 0:
                        act.wait_ge(xT_psum, 4 * n + k // 2 + 1)
                    a = act.activation(xh[:, k, :], ps[:, b0 + k // 2, (k % 2) * SEQ:(k % 2 + 1) * SEQ], ACT.Copy,
                                       scale=col(gain, k))
                    if k % 2:
                        a.then_inc(xh_ready, 1)

            act.dma_start(rows_in[0:2 * KD, :], ln_mix.rearrange("l (k p) -> (l k) p", p=P)).then_inc(mix_landed, 16)
            act.wait_ge(prm_ready, 1)
            norm_hi(0, MIX, 0)
            split_dense(1)
            act.wait_ge(x_in, 16)
            act.wait_ge(x_in1, 16)
            squares(lambda t: region[:, 512 + D * t:512 + D * (t + 1)])
            split_dense(HI_RING)
            root(0)
            act.wait_ge(lam_summed, 1)
            act.activation(lam_t[:, 2:4], lam_t[:, 0:2], ACT.Exp).then_inc(lam_exp, 1)
            act.wait_ge(lru_exp, 1)
            act.activation(lru_c[:, 1, :], lru_c[:, 0, :], ACT.Exp, scale=-1.0).then_inc(lru_exp, 1)

            used = lambda name: unit_of[name][-1] + 1
            split_dense(used("k1") + 2)

            def copy_turned(n, banks, dst, c):
                act.wait_ge(rot_psum, n + 1)
                for b in range(2):
                    a = act.activation(dst[:, 4 * c + 2 * b:4 * c + 2 * b + 2, :],
                                       ps[:, banks[b], :].rearrange("p (k t) -> p k t", k=2), ACT.Copy)
                a.then_inc(qk_ready, 1)

            copy_turned(0, (4, 5), kT, 0)
            split_dense(used("q0") + 2)
            copy_turned(1, (6, 7), kT, 1)
            split_dense(used("q1") + 2)
            copy_turned(2, (0, 1), qT, 0)
            split_dense(used("v0") + 2)
            copy_turned(3, (2, 3), qT, 1)
            split_dense(used("v0") + 3)

            def copy_values(c, name):
                act.wait_ge(unit_used, used(name))
                act.wait_ge(rstd_ready, 1)
                for t in range(TB):
                    a = act.activation(v_sb[:, t, c * BANK:(c + 1) * BANK], ps[:, 4 + 2 * c + t, :], ACT.Copy,
                                       scale=ss[:, 6 + t:7 + t])
                a.then_inc(v_ready, 1)

            copy_values(0, "v0")

            def exps(n):
                qb, h0, nh = tiles[n]
                keys = (qb + 1) * P
                act.wait_ge(max_ready, n + 1)
                for m in range(2):
                    for i in range(nh):
                        s = sc_sb[n % 2][:, m, i * keys:(i + 1) * keys]
                        a = act.activation(s, s, ACT.Exp, scale=HD ** -0.5, bias=mx[:, n % 2, m, i:i + 1],
                                           accum_out=den[:, n % 2, m, i:i + 1])
                a.then_inc(exp_ready, 1)

            def turned_weights(n):
                act.wait_ge(wT_psum, n + 1)
                if n >= 2:
                    act.wait_ge(pv_done, n - 1)
                act.activation(wT[n % 2], ps[:, 4 + n % 2, :], ACT.Copy).then_inc(wT_ready, 1)

            def o_squares(i):
                qb, h0, nh, _ = parts[i]
                act.wait_ge(o_copied, i + 1)
                for h in range(h0, h0 + nh):
                    a = act.activation(xh[:, 4 + h // 2 % 4, (h % 2) * P:(h % 2 + 1) * P], xn[:, qb, h * P:(h + 1) * P],
                                       ACT.Square, accum_out=ss_o[:, 2, qb, h:h + 1])
                a.then_inc(o_squared, 1)

            def o_root_of(i):
                qb, h0, nh, _ = parts[i]
                act.wait_ge(o_mean, i + 1)
                act.activation(ss_o[:, 1, qb, h0:h0 + nh], ss_o[:, 0, qb, h0:h0 + nh], ACT.Sqrt).then_inc(o_root, 1)

            def o_hi(half):
                for k in (2 * half, 2 * half + 1):
                    act.wait_ge(oT_psum, k + 1)
                    act.activation(xh[:, 2 * k:2 * k + 2, :], ps[:, k, :].rearrange("p (k t) -> p k t", k=2), ACT.Copy,
                                   scale=gsub[:, 0:1]).then_inc(oh_ready, 1)

            exps(0)
            exps(1)
            split_dense(used("v1") + 2)
            copy_values(1, "v1")
            split_dense(used("v1") + 3)
            turned_weights(0)
            for n in range(2, len(tiles)):
                turned_weights(n - 1)
                exps(n)
                if n == 3:
                    o_squares(0)
                if n == 4:
                    o_root_of(0)
                if n == 5:
                    o_squares(1)
                    o_root_of(1)
            o_hi(0)
            turned_weights(len(tiles) - 1)
            o_squares(2)
            o_root_of(2)
            o_hi(1)
            split_dense(used("o1"))
            act.dma_start(p_in[0], p[0, 0].rearrange("(t p) d -> p t d", p=P)).then_inc(p_landed, 16)
            split_dense(used("o1") + 2)

            act.wait_ge(unit_used, used("o1"))
            act.wait_ge(prm_ready, 2)
            norm_hi(1, FFN, 0)
            act.wait_ge(res_added, 4)
            split_dense(used("g0"))
            squares()
            root(1)
            for j in range(FSTEPS):
                w = fwidth[j]
                split_dense(used(f"g{j}") + 2)
                act.wait_ge(unit_used, used(f"g{j}"))
                if j:
                    act.wait_ge(hT_psum, TB * j)
                else:
                    act.wait_ge(rstd_ready, 2)
                for t in range(TB):
                    act.activation(hid[:, t, 0:w], ps[:, 2 * (j % 2) + t, 0:w], ACT.Silu,
                                   scale=ss[:, 6 + t:7 + t]).then_inc(silu_done, 1)
                split_dense((used(f"d{j - 1}") if j else used("u0")) + 2)
                for t in range(TB):
                    act.wait_ge(hT_psum, TB * j + t + 1)
                    act.activation(hTh[:, 0:w // P, t * P:(t + 1) * P],
                                   ps[:, 2 * (j % 2) + t, 0:w].rearrange("p (k t) -> p k t", t=P),
                                   ACT.Copy).then_inc(hTh_ready, 1)
            def embedding_in(layer):
                act.wait_ge(pT_psum, layer + 1)
                act.activation(pTh[layer], ps[:, layer, :].rearrange("p (k t) -> p k t", k=KP), ACT.Copy).then_inc(pTh_ready, 1)

            act.wait_ge(unit_used, used(f"d{FSTEPS - 2}"))
            embedding_in(0)
            split_dense(used(f"d{FSTEPS - 1}") + 2)

            def embedding_gate(c, used_to, added):
                act.wait_ge(unit_used, used_to)
                if c:
                    act.wait_ge(res_added, added + TB)
                for t in range(TB):
                    act.activation(sig[:, t, :], ps[:, 4 + 2 * c + t, :], ACT.Sigmoid,
                                   scale=ss[:, 6 + t:7 + t]).then_inc(gate_ready, 1)

            act.wait_ge(res_added, 8)
            norm_hi(2, PLE, 4)
            split_dense(used("pg0"))
            squares()
            root(2)
            split_dense(used("pg0") + 2)
            act.wait_ge(rstd_ready, 3)
            embedding_gate(0, used("pg0"), 8)
            split_dense(used("pg1") + 1)
            half_squares(0, 8)
            split_dense(used("pg1") + 2)
            embedding_gate(1, used("pg1"), 8)
            half_squares(1, 8)

            root(3)
            norm_hi(3, MIX + 1, 4)

            def conv_in(c, name):
                act.wait_ge(unit_used, used(name))
                if c == 0:
                    act.wait_ge(xp_zero, 1)
                else:
                    act.wait_ge(conv_ready, 1)
                b0 = 4 * c
                for b in range(4):
                    k = 4 * c + b
                    act.activation(u_half[c][:, b, :], ps[:, b0 + b, 0:SEQ], ACT.Identity, scale=col(CW + CONV - 1, k),
                                   bias=col(CB, k))
                act.activation(xp[:, :, CONV - 1:], ps[:, b0:b0 + 4, 0:SEQ], ACT.Copy).then_inc(xp_ready, 1)

            def conv_out(c):
                act.wait_ge(conv_ready, c + 1)
                if c:
                    act.wait_ge(unit_used, used("ga0"))
                act.activation(uh, u_half[c], ACT.Copy).then_inc(uh_ready, 1)

            def gates(c):
                act.wait_ge(unit_used, used(f"ga{c}"))
                for b in range(4):
                    a = act.activation(lru_i[c][:, b, :], ps[:, b, SEQ:2 * SEQ], ACT.Sigmoid, bias=col(BX, 4 * c + b))
                a.then_inc(in_gate_ready, 1)
                for b in range(4):
                    a = act.activation(lru_r[c][:, b, :], ps[:, b, 0:SEQ], ACT.Sigmoid, bias=col(BA, 4 * c + b))
                a.then_inc(sig_ready, 1)

            def decays(c):
                act.wait_ge(sig_ready, c + 1)
                if c:
                    act.wait_ge(scan_read, 2)
                for b in range(4):
                    act.activation(lru_h[:, 4 * c + b, :], lru_r[c][:, b, :], ACT.Exp, scale=lru_c[:, 3, 4 * c + b:4 * c + b + 1])

            def tanhs(c):
                for b in range(4):
                    a = act.activation(lru_r[c][:, b, :], lru_r[c][:, b, :], ACT.Tanh, scale=lru_c[:, 5, 4 * c + b:4 * c + b + 1])
                a.then_inc(tanh_ready, 1)
                act.wait_ge(tanh_ready, c + 1)
                if c:
                    act.wait_ge(scan_in, 1)
                act.activation(sq_half, lru_r[c], ACT.Sqrt).then_inc(sqrt_ready, 1)

            def gelu(c):
                act.wait_ge(unit_used, used(f"y{c}"))
                if c:
                    act.wait_ge(scan_ready, 1)
                else:
                    act.wait_ge(scan_read, 1)
                act.activation(lru_y[c], ps[:, 4:8, 0:SEQ], ACT.Gelu_apprx_tanh).then_inc(gelu_ready, 1)

            def z_hi(c):
                act.wait_ge(z_ready, c + 1)
                act.wait_ge(unit_used, used("y1") - 1 + c)
                for k in (4 * c, 4 * c + 2):
                    act.activation(xh[:, k:k + 2, :], lru_h[:, k:k + 2, :], ACT.Copy).then_inc(zh_ready, 1)

            split_dense(used("x0") + 2)
            conv_in(0, "x0")
            split_dense(used("x1") + 2)
            conv_out(0)
            conv_in(1, "x1")
            split_dense(used("ga0") + 2)
            act.wait_ge(lru_ready, 1)
            gates(0)
            conv_out(1)
            split_dense(used("y0") + 2)
            decays(0)
            gelu(0)
            split_dense(used("ga1") + 2)
            tanhs(0)
            split_dense(used("y1") + 1)
            gates(1)
            decays(1)
            z_hi(0)
            tanhs(1)
            split_dense(used("y1") + 2)
            gelu(1)
            z_hi(1)
            act.dma_start(p_in[1], p[1, 0].rearrange("(t p) d -> p t d", p=P)).then_inc(p_landed, 16)
            split_dense(used("ro1") + 2)

            act.wait_ge(rw_in, 16)
            act.activation(rw_h[:], rw[:], ACT.Copy).then_inc(rw_h_ready, 1)
            norm_hi(4, FFN + 1, 4)
            act.wait_ge(res_added, 16)
            squares()
            root(4)
            embedding_in(1)
            act.wait_ge(gap_ready, 1)
            act.activation(small[:, 6, :], small[:, 5, :], ACT.Exp).then_inc(gap_exp, 1)
            split_moe(0, 0, HI_RING)

            def gathered_hi(n):
                act.wait_ge(gathered, n + 1)
                for k in range(KD):
                    a = act.activation(xh[:, k, 0:P], ps[:, 6 + k // 4, (k % 4) * P:(k % 4 + 1) * P], ACT.Copy,
                                       scale=col(FFN + 1, k))
                a.then_inc(gh_ready, 1)

            gathered_hi(0)
            act.wait_ge(items_ready, 1)
            extra = act.value_load(ctl[0:1, EXTRA:EXTRA + 1], min_val=0, max_val=EXTRA)
            items = act.snap(extra + E)
            STEPS = FE // CHUNK
            with act.Fori(0, items) as it:
                done = STEPS * it + TB * FSTEPS
                used_base = U_ITEM * it + U0
                at = HI_RING
                for j in range(STEPS):
                    u = moe_unit[f"g{j}"][-1] + 1
                    split_moe(it, at, u + 2)
                    at = max(at, u + 2)
                    act.wait_ge(unit_used, used_base + u)
                    act.wait_ge(hT_psum, done + j)
                    act.activation(m_hid, ps[:, j % 2, :], ACT.Silu).then_inc(silu_done, 1)
                    u = moe_unit[f"d{j - 1}" if j else "u0"][-1] + 1
                    split_moe(it, at, u + 2)
                    at = max(at, u + 2)
                    act.wait_ge(hT_psum, done + (j + 1))
                    act.activation(mTh, ps[:, j % 2, :].rearrange("p (k t) -> p k t", t=P), ACT.Copy).then_inc(hTh_ready, 1)
                    if j == 1:
                        act.wait_ge(selT_psum, it + 1)
                        act.activation(sel_gT, ps[:, 2, 0:SEQ], ACT.Copy).then_inc(selT_ready, 1)
                split_moe(it, at, U_ITEM)
                gathered_hi(it + 1)
                split_moe(it + 1, 0, HI_RING - 1)
                act.wait_ge(unit_used, used_base + U_ITEM)
                act.wait_ge(scattered, it + 1)
                act.activation(y_sb[:, 0:BANK], ps[:, 4, :], ACT.Copy).then_inc(y_act, 1)
                split_moe(it + 1, HI_RING - 1, HI_RING)

            act.wait_ge(scattered, items + 1)
            act.dma_start(lnf_row, ln_final.partition_broadcast(P)).then_inc(lnf_in, 16)
            base = U_ITEM * items

            def split_post(first, upto):
                for i in range(first, upto):
                    u = U0 + i
                    s, half = i // 2, i % 2
                    act.wait_ge(landed[s][half], LAND_ITEM * items + (LAND0[s][half] + 16))
                    act.wait_ge(unit_used, base + (u - HI_RING + 1))
                    act.activation(w_hi[:, u % HI_RING, :], raw[:, s, half * UNIT:(half + 1) * UNIT], ACT.Copy).then_inc(hi_done, 1)

            norm_hi(5, PLE + 1, 4)
            act.wait_ge(res_added, 4 * items + 20)
            squares()
            root(5)
            split_post(HI_RING, 4)
            act.wait_ge(rstd_ready, 6)
            embedding_gate(0, base + (U0 + 3), 4 * items + 20)
            split_post(4, 5)
            half_squares(0, 4 * items + 20)
            embedding_gate(1, base + (U0 + 5), 4 * items + 20)
            half_squares(1, 4 * items + 20)
            root(6)

        @block.vector
        def _(dve):
            chain = [0]

            def link(ins):
                chain[0] += 1
                ins.then_inc(dve_chain, 1)
                dve.wait_ge(dve_chain, chain[0])

            class split:
                at = 0

            def split_dense(upto):
                while split.at < min(upto, U0):
                    u = split.at
                    split.at += 1
                    name, off, n = unit_shape[u]
                    dve.wait_ge(hi_done, u + 1)
                    if u >= LO_RING:
                        dve.wait_ge(unit_used, u - LO_RING + 1)
                    dve.tensor_tensor(w_lo[:, u % LO_RING, 0:n], raw[:, slot_of[name], off:off + n],
                                      w_hi[:, u % HI_RING, 0:n].bitcast(F32), ALU.subtract).then_inc(lo_done, 1)

            def split_moe(it, first, upto):
                for u in range(first, min(upto, U_ITEM)):
                    s = moe_slot[u // 2]
                    off = (u % 2) * UNIT
                    dve.wait_ge(hi_done, U_ITEM * it + (U0 + u + 1))
                    dve.wait_ge(unit_used, U_ITEM * it + (U0 + u - LO_RING + 1))
                    dve.tensor_tensor(w_lo[:, (U0 + u) % LO_RING, :], raw[:, s, off:off + UNIT],
                                      w_hi[:, (U0 + u) % HI_RING, :].bitcast(F32), ALU.subtract).then_inc(lo_done, 1)

            def rest(out, psum, gain, rounded):
                return dve.scalar_tensor_tensor(out=out, in0=psum, scalar=gain, in1=rounded.bitcast(F32),
                                                op0=ALU.mult, op1=ALU.subtract)

            after_squares = (2, 4, 6, 10, 12, 14, 18)

            def mean(n):
                dve.wait_ge(squared, after_squares[n])
                if n in (3, 6):
                    link(dve.tensor_tensor(ss[:, 0:2], ss_half[:, 0, :], ss_half[:, 1, :], ALU.add))
                dve.tensor_scalar(ss[:, 2:4], ss[:, 0:2], 1.0 / D, EPS, ALU.mult, ALU.add).then_inc(mean_ready, 1)

            def rstd(n):
                dve.wait_ge(root_ready, n + 1)
                dve.reciprocal(ss[:, 6:8], ss[:, 4:6]).then_inc(rstd_ready, 1)
                dve.wait_ge(rstd_ready, n + 1)

            def scale_tokens():
                for t in range(TB):
                    dve.tensor_scalar(xn[:, t, :], res[:, t, :], ss[:, 6 + t:7 + t], None, ALU.mult).then_inc(xn_ready, 1)

            def norm_lo(n, gain, b0):
                for k in range(KD):
                    if k % 2 == 0:
                        dve.wait_ge(xh_ready, 4 * n + k // 2 + 1)
                    a = rest(xl[:, k, :], ps[:, b0 + k // 2, (k % 2) * SEQ:(k % 2 + 1) * SEQ], col(gain, k), xh[:, k, :])
                    if k % 2:
                        a.then_inc(xl_ready, 1)

            def add_residual(b, t, n):
                dve.tensor_tensor(res[:, t, n * BANK:(n + 1) * BANK], res[:, t, n * BANK:(n + 1) * BANK],
                                  ps[:, b, :], ALU.add).then_inc(res_added, 1)

            used = lambda name: unit_of[name][-1] + 1

            dve.wait_ge(prm_psum, 1)
            dve.tensor_copy(prm[:, 0:2 * KD], ps[:, 7, 0:2 * KD]).then_inc(prm_ready, 1)
            dve.wait_ge(prm_ready, 1)
            norm_lo(0, MIX, 0)
            split_dense(1)
            dve.wait_ge(prm_psum, 2)
            dve.tensor_copy(prm[:, 2 * KD:], ps[:, 7, 2 * KD:N_ROWS]).then_inc(prm_ready, 1)
            dve.wait_ge(prm_ready, 2)
            split_dense(LO_RING)
            mean(0)
            dve.wait_ge(lam_landed, 64)
            link(dve.tensor_tensor(lam_in[:, 0:2, :], lam_in[:, 0:2, :], lam_in[:, 2:4, :], ALU.mult))
            dve.tensor_reduce(lam_t[:, 0:2], lam_in[:, 0:2, :], AX.X, ALU.add).then_inc(lam_summed, 1)
            rstd(0)
            dve.wait_ge(rope_in, 16)
            for t in range(TB):
                a = dve.tensor_scalar(rope_sb[:, t], rope_sb[:, t], ss[:, 6 + t:7 + t], None, ALU.mult)
            link(a)
            link(dve.tensor_scalar(gsub[:], SUB, 1.0 - LAMBDA_INIT, None, ALU.mult))
            lamb = prm[:, LAM * KD:(LAM + 1) * KD]
            dve.scalar_tensor_tensor(out=lru_c[:, 0, :], in0=lamb, scalar=-1.0, in1=lamb, op0=ALU.mult,
                                     op1=ALU.max).then_inc(lru_exp, 1)
            split_dense(used("k0") + 1)
            dve.wait_ge(lam_exp, 1)
            link(dve.tensor_tensor(lam_t[:, 5:6], lam_t[:, 3:4], lam_t[:, 2:3], ALU.subtract))
            dve.tensor_scalar(lam_t[:, 4:5], lam_t[:, 5:6], LAMBDA_INIT, None, ALU.subtract).then_inc(lam_ready, 1)
            def lru_constants():
                dve.wait_ge(lru_exp, 2)
                z, s, s2, poly = lru_c[:, 1, :], lru_c[:, 2, :], lru_c[:, 3, :], lru_c[:, 4, :]
                link(dve.tensor_scalar(s, z, 2.0, None, ALU.add))
                link(dve.reciprocal(s, s))
                link(dve.tensor_tensor(s, s, z, ALU.mult))
                link(dve.tensor_tensor(s2, s, s, ALU.mult))
                link(dve.tensor_scalar(poly, s2, 1.0 / 17, None, ALU.mult))
                for n in range(15, 1, -2):
                    link(dve.scalar_tensor_tensor(out=poly, in0=poly, scalar=1.0 / n, in1=s2, op0=ALU.add, op1=ALU.mult))
                link(dve.scalar_tensor_tensor(out=poly, in0=poly, scalar=1.0, in1=s, op0=ALU.add, op1=ALU.mult))
                link(dve.tensor_scalar(lru_c[:, 5, :], lamb, -4.0, 0.0, ALU.mult, ALU.max))
                link(dve.scalar_tensor_tensor(out=lru_c[:, 5, :], in0=poly, scalar=8.0, in1=lru_c[:, 5, :],
                                              op0=ALU.mult, op1=ALU.add))
                dve.tensor_scalar(s2, lru_c[:, 5, :], -2.0, None, ALU.mult).then_inc(lru_ready, 1)

            def rotate(n, name, banks):
                dve.wait_ge(unit_used, used(name))
                for t in range(TB):
                    if n:
                        dve.wait_ge(rot_ready, TB * (n - 1) + t + 1)
                    halves = ps[:, banks[t], :].rearrange("p (h a f) -> p h a f", a=2, f=HD // 2)
                    out_b = rot_b[:, t, :].rearrange("p (h a f) -> p h a f", a=2, f=HD // 2)
                    cos_t, sin_t, nsin_t = (rope_sb[:, t, i, :].unsqueeze(1) for i in range(3))
                    dve.tensor_tensor(rot_a[:, t, :].rearrange("p (g f) -> p g f", f=HD // 2),
                                      ps[:, banks[t], :].rearrange("p (g f) -> p g f", f=HD // 2),
                                      cos_t.broadcast_to([P, 2 * 8, HD // 2]), ALU.mult)
                    dve.tensor_tensor(out_b[:, :, 0, :], halves[:, :, 1, :], nsin_t.broadcast_to([P, 8, HD // 2]), ALU.mult)
                    dve.tensor_tensor(out_b[:, :, 1, :], halves[:, :, 0, :], sin_t.broadcast_to([P, 8, HD // 2]),
                                      ALU.mult).then_inc(rot_parts, 1)

            rotate(0, "k0", (4, 5))
            split_dense(used("k1") + 1)
            rotate(1, "k1", (6, 7))
            split_dense(used("q0") + 1)
            rotate(2, "q0", (0, 1))
            split_dense(used("q1") + 1)
            rotate(3, "q1", (2, 3))
            split_dense(used("v0") + 1)

            def mask_and_max(n):
                qb, h0, nh = tiles[n]
                keys = (qb + 1) * P
                s_n, mx_n = sc_sb[n % 2], mx[:, n % 2, :, 0:nh]
                dve.wait_ge(scored, n + 1)
                if n >= 2:
                    dve.wait_ge(wT_psum, n - 1)
                m3 = mask[:].unsqueeze(1).broadcast_to([P, nh, P])
                for m in range(2):
                    dst = s_n[:, m, :].rearrange("p (h k) -> p h k", h=nh)
                    src = ps[:, 2 * (n % 2) + m, :].rearrange("p (h k) -> p h k", h=nh)
                    if qb:
                        dve.tensor_copy(dst[:, :, 0:qb * P], src[:, :, 0:qb * P])
                    a = dve.tensor_tensor(dst[:, :, qb * P:keys], src[:, :, qb * P:keys], m3, ALU.add)
                a.then_inc(masked, 1)
                dve.wait_ge(masked, n + 1)
                for m in range(2):
                    a = dve.tensor_reduce(mx[:, n % 2, m, 0:nh], s_n[:, m, :].rearrange("p (h k) -> p h k", h=nh), AX.X, ALU.max)
                link(a)
                dve.tensor_scalar(mx_n, mx_n, -(HD ** -0.5), None, ALU.mult).then_inc(max_ready, 1)

            def weigh(n):
                qb, h0, nh = tiles[n]
                keys = (qb + 1) * P
                part = lambda m, i: sc_sb[n % 2][:, m, i * keys:(i + 1) * keys]
                r = rden[:, n % 2]
                dve.wait_ge(exp_ready, n + 1)
                link(dve.reciprocal(r[:, :, 0:nh], den[:, n % 2, :, 0:nh]))
                link(dve.tensor_scalar(r[:, 1, 0:nh], r[:, 1, 0:nh], nlam[:, 0:1], None, ALU.mult))
                for i in range(nh):
                    a = dve.tensor_scalar(part(1, i), part(1, i), r[:, 1, i:i + 1], None, ALU.mult)
                link(a)
                for i in range(nh):
                    a = dve.scalar_tensor_tensor(out=part(0, i), in0=part(0, i), scalar=r[:, 0, i:i + 1],
                                                 in1=part(1, i), op0=ALU.mult, op1=ALU.add)
                a.then_inc(weighed, 1)

            def o_copy(i):
                qb, h0, nh, before = parts[i]
                dve.wait_ge(pv_done, before)
                for b in range(h0 // 4, (h0 + nh) // 4):
                    a = dve.tensor_copy(xn[:, qb, b * BANK:(b + 1) * BANK], ps[:, 6 + b, :])
                a.then_inc(o_copied, 1)

            def o_mean_of(i):
                qb, h0, nh, _ = parts[i]
                dve.wait_ge(o_squared, i + 1)
                dve.tensor_scalar(ss_o[:, 0, qb, h0:h0 + nh], ss_o[:, 2, qb, h0:h0 + nh], 1.0 / P, SUB_EPS,
                                  ALU.mult, ALU.add).then_inc(o_mean, 1)

            def o_normalise(i):
                qb, h0, nh, _ = parts[i]
                dve.wait_ge(o_root, i + 1)
                link(dve.reciprocal(ss_o[:, 2, qb, h0:h0 + nh], ss_o[:, 1, qb, h0:h0 + nh]))
                dve.wait_ge(o_copied, i + 1)
                o3 = xn[:, qb, h0 * P:(h0 + nh) * P].rearrange("p (h e) -> p h e", h=nh)
                dve.tensor_tensor(o3, o3, ss_o[:, 2, qb, h0:h0 + nh].unsqueeze(2).broadcast_to([P, nh, P]),
                                  ALU.mult).then_inc(o_ready, 1)

            def o_lo(half):
                for k in (2 * half, 2 * half + 1):
                    dve.wait_ge(oh_ready, k + 1)
                    rest(xl[:, 2 * k:2 * k + 2, :], ps[:, k, :].rearrange("p (k t) -> p k t", k=2), gsub[:, 0:1],
                         xh[:, 2 * k:2 * k + 2, :]).then_inc(ol_ready, 1)

            mask_and_max(0)
            dve.wait_ge(lam_psum, 1)
            dve.tensor_copy(nlam[:], ps[:, 6, 0:1]).then_inc(nlam_ready, 1)
            mask_and_max(1)
            split_dense(used("v1") + 1)
            dve.wait_ge(nlam_ready, 1)
            weigh(0)
            for n in range(1, len(tiles)):
                if n == 5:
                    o_mean_of(1)
                weigh(n)
                if n + 1 < len(tiles):
                    mask_and_max(n + 1)
                if n == 1:
                    o_copy(0)
                if n == 2:
                    split_dense(used("o0"))
                if n == 3:
                    o_mean_of(0)
                if n == 4:
                    o_copy(1)
                    o_normalise(0)
            o_normalise(1)
            o_lo(0)
            o_copy(2)
            o_mean_of(2)
            o_normalise(2)
            o_lo(1)
            for c in range(2):
                split_dense(used(f"o{c}") + 1)
                dve.wait_ge(unit_used, used(f"o{c}"))
                for t in range(TB):
                    add_residual(4 + 2 * c + t, t, c)

            norm_lo(1, FFN, 0)
            split_dense(used("o1") + 2)
            mean(1)
            rstd(1)
            for j in range(FSTEPS):
                w = fwidth[j]
                split_dense(used(f"u{j}") + 1)
                dve.wait_ge(unit_used, used(f"u{j}"))
                for t in range(TB):
                    dve.wait_ge(silu_done, TB * j + t + 1)
                    dve.scalar_tensor_tensor(out=hid[:, t, 0:w], in0=ps[:, 2 * (1 - j % 2) + t, 0:w],
                                             scalar=ss[:, 6 + t:7 + t], in1=hid[:, t, 0:w], op0=ALU.mult,
                                             op1=ALU.mult).then_inc(hid_ready, 1)
                if j:
                    split_dense(used(f"d{j - 1}") + 1)
                if j == 1:
                    lru_constants()
                for t in range(TB):
                    dve.wait_ge(hTh_ready, TB * j + t + 1)
                    dve.tensor_tensor(hTl[:, 0:w // P, t * P:(t + 1) * P],
                                      ps[:, 2 * (j % 2) + t, 0:w].rearrange("p (k t) -> p k t", t=P),
                                      hTh[:, 0:w // P, t * P:(t + 1) * P].bitcast(F32), ALU.subtract).then_inc(hTl_ready, 1)
            def embedding_rest(layer):
                dve.wait_ge(pTh_ready, layer + 1)
                dve.tensor_tensor(pTl[layer], ps[:, layer, :].rearrange("p (k t) -> p k t", k=KP), pTh[layer].bitcast(F32),
                                  ALU.subtract).then_inc(pTl_ready, 1)

            embedding_rest(0)
            split_dense(used(f"d{FSTEPS - 1}") + 1)
            dve.wait_ge(unit_used, used(f"d{FSTEPS - 1}"))
            for n in range(2):
                for t in range(TB):
                    add_residual(4 + 2 * n + t, t, n)

            def embedding_sum(layer, between):
                for c in range(2):
                    for t in range(TB):
                        dve.wait_ge(gate_ready, TB * (2 * layer + c) + t + 1)
                        link(dve.tensor_tensor(sig[:, t, :], sig[:, t, :], ps[:, 2 * t + c, :], ALU.mult))
                        r = res[:, t, c * BANK:(c + 1) * BANK]
                        dve.tensor_tensor(r, r, sig[:, t, :], ALU.add).then_inc(res_added, 1)
                    if c == 0:
                        between()

            split_dense(used("pp") + 1)
            norm_lo(2, PLE, 4)
            split_dense(used("pg0"))
            mean(2)
            rstd(2)
            split_dense(used("pg0") + 1)
            embedding_sum(0, lambda: split_dense(used("pg1") + 1))

            mean(3)
            rstd(3)
            for c in range(2):
                for t in range(TB):
                    h = slice(c * BANK, (c + 1) * BANK)
                    dve.tensor_scalar(xn[:, t, h], res[:, t, h], ss[:, 6 + t:7 + t], None, ALU.mult).then_inc(xn_ready, 1)
            norm_lo(3, MIX + 1, 4)

            def conv(c):
                dve.wait_ge(xp_ready, c + 1)
                for i in range(CONV - 1):
                    for b in range(4):
                        a = dve.scalar_tensor_tensor(out=u_half[c][:, b, :], in0=xp[:, b, i:i + SEQ],
                                                     scalar=col(CW + i, 4 * c + b), in1=u_half[c][:, b, :],
                                                     op0=ALU.mult, op1=ALU.add)
                    if i < CONV - 2:
                        link(a)
                a.then_inc(conv_ready, 1)

            def conv_lo(c):
                dve.wait_ge(uh_ready, c + 1)
                dve.tensor_tensor(ul, u_half[c], uh.bitcast(F32), ALU.subtract).then_inc(ul_ready, 1)

            def scan(c, between=None):
                g = lru_h[:, 4 * c:4 * c + 4, :]
                r, i_u = lru_r[c], lru_iu[c]
                dve.wait_ge(scan_read, c + 1)
                dve.wait_ge(sqrt_ready, c + 1)
                link(dve.tensor_scalar(g, g, 1.0, None, ALU.add))
                link(dve.scalar_tensor_tensor(out=r, in0=r, scalar=1.0, in1=g, op0=ALU.add, op1=ALU.mult))
                link(dve.scalar_tensor_tensor(out=r, in0=r, scalar=-4.0, in1=g, op0=ALU.add, op1=ALU.mult))
                link(dve.scalar_tensor_tensor(out=sq_half, in0=r, scalar=-0.5, in1=sq_half, op0=ALU.mult, op1=ALU.mult))
                dve.tensor_scalar(r, r, -0.5, -1.0, ALU.mult, ALU.add)
                dve.tensor_tensor(i_u, sq_half, i_u, ALU.mult).then_inc(scan_in, 1)
                if between:
                    between()
                dve.wait_ge(scan_in, c + 1)
                for b in range(4):
                    a = dve.tensor_tensor_scan(lru_h[:, 4 * c + b, :], r[:, b, :], i_u[:, b, :], 0.0, ALU.mult, ALU.add)
                a.then_inc(scan_ready, 1)

            def z_of(c):
                dve.wait_ge(scan_ready, c + 1)
                dve.wait_ge(gelu_ready, c + 1)
                z = lru_h[:, 4 * c:4 * c + 4, :]
                dve.tensor_tensor(z, z, lru_y[c], ALU.mult).then_inc(z_ready, 1)

            def z_lo(c):
                for k in (4 * c, 4 * c + 2):
                    dve.wait_ge(zh_ready, k // 2 + 1)
                    dve.tensor_tensor(xl[:, k:k + 2, :], lru_h[:, k:k + 2, :], xh[:, k:k + 2, :].bitcast(F32),
                                      ALU.subtract).then_inc(zl_ready, 1)

            split_dense(used("x0") + 2)
            conv(0)
            split_dense(used("x1") + 1)
            conv_lo(0)
            split_dense(used("ga0") + 1)
            conv(1)
            split_dense(used("ga0") + 2)
            conv_lo(1)
            split_dense(used("y0") + 2)
            split_dense(used("ga1") + 2)
            scan(0)
            z_of(0)
            z_lo(0)
            split_dense(used("y1") + 1)
            scan(1, lambda: split_dense(used("y1") + 2))
            z_of(1)
            z_lo(1)
            split_dense(used("ro1") + 1)
            dve.wait_ge(unit_used, used("ro1"))
            for n in range(2):
                for t in range(TB):
                    add_residual(2 * n + t, t, n)

            dve.wait_ge(rw_h_ready, 1)
            dve.tensor_tensor(rw_l[:], rw[:], rw_h[:].bitcast(F32), ALU.subtract).then_inc(rw_l_ready, 1)
            norm_lo(4, FFN + 1, 4)
            dve.wait_ge(logitT_psum, 1)
            dve.tensor_copy(logitT, ps[0:E, 0, 0:SEQ]).then_inc(logitT_ready, 1)
            logit, eq, one, second, chose, gate, left, rank = (route[:, i] for i in range(8))
            top1, top2, m = small[:, 0, :], small[:, 1, :], small[:, 2, :]
            wide = lambda a: a.unsqueeze(2).broadcast_to([P, TB, E])

            def one_hots(n):
                one = bass.ds(n, 1)
                dve.tensor_copy(cur[:, 0:TB].unsqueeze(2), item_pos[:, :, one])
                dve.tensor_copy(cur[:, TB:2 * TB].unsqueeze(2), item_gate[:, :, one]).then_inc(cur_ready, 1)
                dve.wait_ge(cur_ready, n + 1)
                for t in range(TB):
                    dve.tensor_scalar(sel[:, t, :], iota_row[:], cur[:, t:t + 1], None, ALU.is_equal)
                    a = dve.tensor_scalar(sel_g[:, t, :], iota_row[:], cur[:, t:t + 1], cur[:, TB + t:TB + t + 1],
                                          ALU.is_equal, ALU.mult)
                a.then_inc(sel_ready, 1)

            def first_of_max(values, best, onehot):
                link(dve.tensor_reduce(best, values, AX.X, ALU.max))
                link(dve.tensor_tensor(eq, values, wide(best), ALU.is_equal))
                link(dve.tensor_tensor(eq, eq, rev[:], ALU.mult))
                link(dve.tensor_reduce(m, eq, AX.X, ALU.max))
                link(dve.tensor_tensor(onehot, eq, wide(m), ALU.is_equal))

            dve.wait_ge(logits_ready, 1)
            link(dve.tensor_copy(logit, ps[:, 5, 0:TB * E].rearrange("p (t e) -> p t e", t=TB)))
            first_of_max(logit, top1, one)
            link(dve.scalar_tensor_tensor(out=left, in0=one, scalar=NEG, in1=logit, op0=ALU.mult, op1=ALU.add))
            first_of_max(left, top2, second)
            dve.tensor_tensor(chose, one, second, ALU.add).then_inc(chosen, 1)
            mean(4)
            rstd(4)
            link(dve.tensor_tensor(small[:, 5, :], top2, top1, ALU.subtract))
            dve.tensor_tensor(small[:, 5, :], small[:, 5, :], ss[:, 6:8], ALU.mult).then_inc(gap_ready, 1)
            scale_tokens()
            dve.wait_ge(gap_exp, 1)
            link(dve.tensor_scalar(small[:, 7, :], small[:, 6, :], 1.0, None, ALU.add))
            link(dve.reciprocal(small[:, 7, :], small[:, 7, :]))
            link(dve.tensor_tensor(small[:, 6, :], small[:, 6, :], small[:, 7, :], ALU.mult))
            link(dve.tensor_tensor(gate, one, wide(small[:, 7, :]), ALU.mult))
            link(dve.tensor_tensor(eq, second, wide(small[:, 6, :]), ALU.mult))
            link(dve.tensor_tensor(gate, gate, eq, ALU.add))
            dve.wait_ge(ranked, 1)
            link(dve.tensor_copy(rank, ps[:, 6:8, 0:E]))
            link(dve.scalar_tensor_tensor(out=rank, in0=rank, scalar=1.0, in1=chose, op0=ALU.add, op1=ALU.mult))
            link(dve.tensor_scalar(rank, rank, -1.0, None, ALU.add))
            dve.tensor_copy(item_pos[:, :, 0:E], rank)
            link(dve.tensor_copy(item_gate[:, :, 0:E], gate))
            one_hots(0)
            split_moe(0, 0, 1)
            full, number, pick, lst = over[:, 0, :], over[:, 1, :], over[:, 2, :], over[:, 3, :]
            link(dve.tensor_scalar(full, ps[:, 5, 0:E], float(P), None, ALU.is_gt))
            link(dve.tensor_tensor_scan(number, ones[:, 0:E], full, 0.0, ALU.mult, ALU.add))
            dve.tensor_copy(ctl_f[:, EXTRA:EXTRA + 1], number[:, E - 1:E])
            dve.memset(item_pos[:, :, ITEMS:], -1.0)
            dve.memset(item_gate[:, :, ITEMS:], 0.0)
            for i in range(EXTRA):
                link(dve.scalar_tensor_tensor(out=pick, in0=number, scalar=float(i + 1), in1=full,
                                              op0=ALU.is_equal, op1=ALU.mult))
                link(dve.scalar_tensor_tensor(out=lst, in0=rev[:, 0, :], scalar=float(E), in1=pick,
                                              op0=ALU.subtract, op1=ALU.mult))
                link(dve.tensor_reduce(ctl_f[:, i:i + 1], lst, AX.X, ALU.add))
                wide_pick = pick.unsqueeze(1).broadcast_to([P, TB, E])
                link(dve.tensor_tensor(eq, rank, wide_pick, ALU.mult))
                link(dve.tensor_reduce(item_pos[:, :, E + i], eq, AX.X, ALU.add))
                link(dve.tensor_tensor(eq, gate, wide_pick, ALU.mult))
                link(dve.tensor_reduce(item_gate[:, :, E + i], eq, AX.X, ALU.add))
            link(dve.tensor_scalar(item_pos[:, :, E:ITEMS], item_pos[:, :, E:ITEMS], -float(P), None, ALU.add))
            link(dve.tensor_scalar(ctl_f[:, 0:EXTRA], ctl_f[:, 0:EXTRA], -1.0, None, ALU.mult))
            dve.tensor_copy(ctl[:], ctl_f[:]).then_inc(items_ready, 1)

            def gathered_lo(n):
                dve.wait_ge(gh_ready, n + 1)
                for k in range(KD):
                    a = rest(xl[:, k, 0:P], ps[:, 6 + k // 4, (k % 4) * P:(k % 4 + 1) * P], col(FFN + 1, k),
                             xh[:, k, 0:P])
                a.then_inc(gl_ready, 1)

            def add_scattered(n):
                dve.wait_ge(scattered, n + 1)
                dve.wait_ge(res_added, 4 * n + 16)
                for c in range(2):
                    for t in range(TB):
                        add_residual(scatter_banks[2 * t + c], t, c)

            embedding_rest(1)
            gathered_lo(0)
            split_moe(0, 1, LO_RING)
            dve.wait_ge(items_ready, 1)
            extra = dve.value_load(ctl[0:1, EXTRA:EXTRA + 1], min_val=0, max_val=EXTRA)
            items = dve.snap(extra + E)
            STEPS = FE // CHUNK
            with dve.Fori(0, items) as it:
                done = STEPS * it + TB * FSTEPS
                used_base = U_ITEM * it + U0
                at = LO_RING
                for j in range(STEPS):
                    u = moe_unit[f"u{j}"][-1] + 1
                    split_moe(it, at, u + 1)
                    at = max(at, u + 1)
                    dve.wait_ge(unit_used, used_base + u)
                    dve.wait_ge(silu_done, done + (j + 1))
                    dve.tensor_tensor(m_hid, m_hid, ps[:, 1 - j % 2, :], ALU.mult).then_inc(hid_ready, 1)
                    if j:
                        u = moe_unit[f"d{j - 1}"][-1] + 1
                        split_moe(it, at, u + 1)
                        at = max(at, u + 1)
                    dve.wait_ge(hTh_ready, done + (j + 1))
                    dve.tensor_tensor(mTl, ps[:, j % 2, :].rearrange("p (k t) -> p k t", t=P), mTh.bitcast(F32),
                                      ALU.subtract).then_inc(hTl_ready, 1)
                    if j == 0:
                        add_scattered(it)
                    if j == 2:
                        dve.wait_ge(selT_psum, it + 1)
                        one_hots(it + 1)
                split_moe(it, at, U_ITEM)
                gathered_lo(it + 1)
                split_moe(it + 1, 0, 1)
                dve.wait_ge(unit_used, used_base + U_ITEM)
                dve.wait_ge(scattered, it + 1)
                dve.tensor_copy(y_sb[:, BANK:D], ps[:, 5, :]).then_inc(y_dve, 1)
                split_moe(it + 1, 1, LO_RING)
            add_scattered(items)

            base = U_ITEM * items

            def split_post(first, upto):
                for i in range(first, upto):
                    u = U0 + i
                    s, off = i // 2, i % 2 * UNIT
                    dve.wait_ge(hi_done, base + (u + 1))
                    dve.wait_ge(unit_used, base + (u - LO_RING + 1))
                    dve.tensor_tensor(w_lo[:, u % LO_RING, :], raw[:, s, off:off + UNIT],
                                      w_hi[:, u % HI_RING, :].bitcast(F32), ALU.subtract).then_inc(lo_done, 1)

            norm_lo(5, PLE + 1, 4)
            split_post(LO_RING, 3)
            mean(5)
            rstd(5)
            split_post(3, 4)
            embedding_sum(1, lambda: split_post(4, 5))

            mean(6)
            rstd(6)
            dve.wait_ge(lnf_in, 16)
            for t in range(TB):
                for c in range(2):
                    h = slice(c * BANK, (c + 1) * BANK)
                    dve.scalar_tensor_tensor(out=xn[:, t, h], in0=res[:, t, h], scalar=ss[:, 6 + t:7 + t], in1=lnf_row[:, h],
                                             op0=ALU.mult, op1=ALU.mult).then_inc(final_ready, 1)


def rope_table():
    f32 = np.float32
    inv = f32(1.0) / np.power(f32(10000.0), np.arange(0, HD, 2, dtype=f32) / f32(HD)).astype(f32)
    angle = np.arange(SEQ, dtype=f32)[:, None] * inv[None, :]
    return np.ascontiguousarray(np.stack([np.cos(angle), np.sin(angle), -np.sin(angle)], axis=1).astype(f32))


NAMES = ["x", "p", "ln_mix", "ln_ffn", "ln_ple", "ln_final", "ple_w_proj", "ple_w_gate", "attn_wq", "attn_wk",
         "attn_wv", "attn_wo", "attn_lambda_q1", "attn_lambda_k1", "attn_lambda_q2", "attn_lambda_k2", "attn_subln",
         "ffn_w_gate", "ffn_w_up", "ffn_w_down", "lru_w_in_x", "lru_w_in_y", "lru_conv_w", "lru_conv_b",
         "lru_gate_a_w", "lru_gate_a_b", "lru_gate_x_w", "lru_gate_x_b", "lru_lambda", "lru_w_out", "moe_w_router",
         "moe_w_gate", "moe_w_up", "moe_w_down"]


def kernel(**inputs):
    import concourse.bacc as bacc
    from concourse.bass_utils import run_bass_kernel_spmd

    nc = bacc.Bacc("TRN2", target_bir_lowering=False, num_devices=1)
    arrays, args = {}, {}
    for name in NAMES:
        arrays[f"in_{name}"] = np.ascontiguousarray(inputs[name])
    arrays["in_rope"] = rope_table()
    for name, a in arrays.items():
        args[name[3:]] = nc.dram_tensor(name, a.shape, mybir.dt.from_np(a.dtype), kind="ExternalInput").ap()
    args["out"] = nc.dram_tensor("out_0", (1, SEQ, D), F32, kind="ExternalOutput").ap()
    build(nc, **args)
    r = run_bass_kernel_spmd(nc, [arrays], core_ids=[0])
    return r.results[0]["out_0"]
```
